# Optimizing a Trainium2 kernel written in Bass

```python
import math
import jax, jax.numpy as jnp
from jax import lax
import numpy as np

D_MODEL = 2048
BATCH = 1
SEQ = 256
DEPTH = 1

DIFF_HEADS = 8
DIFF_HEAD_DIM = 64
DIFF_V_DIM = 2 * DIFF_HEAD_DIM
DIFF_WIDTH = DIFF_HEADS * DIFF_V_DIM
SWA_Q_HEADS = 16
SWA_KV_HEADS = 4
SWA_GROUP = SWA_Q_HEADS // SWA_KV_HEADS
SWA_HEAD_DIM = 64
SWA_WIDTH = SWA_Q_HEADS * SWA_HEAD_DIM
SWA_KV_WIDTH = SWA_KV_HEADS * SWA_HEAD_DIM
WINDOW = 128
Q_BLOCK = 128
D_FF = 5504
NORM_EPS = 1e-6
N_BRANCHES = 2
NEG_INF = -1e30
COL_SIZES = (DIFF_WIDTH, DIFF_WIDTH, DIFF_WIDTH, SWA_WIDTH, SWA_KV_WIDTH, SWA_KV_WIDTH, N_BRANCHES * D_MODEL)
IN_COLS = DIFF_WIDTH * 3 + SWA_WIDTH + 2 * SWA_KV_WIDTH + N_BRANCHES * D_MODEL

kernel_name = "hybrid_diffattn_swa_sink_gated_macaron"

def rmsnorm(x, g):
    xf = x.astype(jnp.float32)
    y = xf * lax.rsqrt(jnp.mean(xf * xf, axis=-1, keepdims=True) + NORM_EPS)
    return (y * g.astype(jnp.float32)).astype(x.dtype)

def alibi_slopes(n):
    return jnp.asarray(2.0 ** (-8.0 * np.arange(1, n + 1) / n), dtype=jnp.float32)

def swiglu(h, w_in, w_out):
    gu = h @ w_in
    g, u = jnp.split(gu, 2, axis=-1)
    return (jax.nn.silu(g) * u) @ w_out

def diff_attention(q, k, v, lam_params, subln, lam_init):
    B, S = q.shape[0], q.shape[1]
    nb = S // Q_BLOCK
    scale = DIFF_HEAD_DIM ** -0.5
    q = q.reshape(B, S, DIFF_HEADS, 2, DIFF_HEAD_DIM) * scale
    k = k.reshape(B, S, DIFF_HEADS, 2, DIFF_HEAD_DIM)
    v = v.reshape(B, S, DIFF_HEADS, DIFF_V_DIM)
    lp = lam_params.astype(jnp.float32)
    lam = jnp.exp(jnp.sum(lp[0] * lp[1])) - jnp.exp(jnp.sum(lp[2] * lp[3])) + lam_init
    slopes = alibi_slopes(DIFF_HEADS)
    k_pos = jnp.arange(S, dtype=jnp.int32)
    qb = jnp.moveaxis(q.reshape(B, nb, Q_BLOCK, DIFF_HEADS, 2, DIFF_HEAD_DIM), 1, 0)

    def body(args):
        qi, i = args
        s = jnp.einsum('bqhcd,bkhcd->bhcqk', qi, k).astype(jnp.float32)
        q_pos = i * Q_BLOCK + jnp.arange(Q_BLOCK, dtype=jnp.int32)
        dist_i = q_pos[:, None] - k_pos[None, :]
        dist = dist_i.astype(jnp.float32)
        bias = -slopes[:, None, None, None] * dist
        s = jnp.where(dist_i >= 0, s + bias, NEG_INF)
        p = jax.nn.softmax(s, axis=-1)
        a = p[:, :, 0] - lam * p[:, :, 1]
        return jnp.einsum('bhqk,bkhe->bqhe', a.astype(v.dtype), v)

    o = lax.map(body, (qb, jnp.arange(nb, dtype=jnp.int32)))
    o = jnp.moveaxis(o, 0, 1).reshape(B, S, DIFF_HEADS, DIFF_V_DIM)
    o = rmsnorm(o, subln) * (1.0 - lam_init)
    return o.reshape(B, S, DIFF_WIDTH)

def swa_attention(q, k, v, sinks):
    B, S = q.shape[0], q.shape[1]
    nb = S // Q_BLOCK
    scale = SWA_HEAD_DIM ** -0.5
    qb = (q * scale).reshape(B, nb, Q_BLOCK, SWA_KV_HEADS, SWA_GROUP, SWA_HEAD_DIM)
    kb = k.reshape(B, nb, Q_BLOCK, SWA_KV_HEADS, SWA_HEAD_DIM)
    vb = v.reshape(B, nb, Q_BLOCK, SWA_KV_HEADS, SWA_HEAD_DIM)
    pad = ((0, 0), (1, 0), (0, 0), (0, 0), (0, 0))
    kk = jnp.concatenate([jnp.pad(kb, pad)[:, :-1], kb], axis=2)
    vv = jnp.concatenate([jnp.pad(vb, pad)[:, :-1], vb], axis=2)
    s = jnp.einsum('bnqkgd,bnskd->bnkgqs', qb, kk).astype(jnp.float32)
    blk = jnp.arange(nb, dtype=jnp.int32)[:, None]
    q_pos = blk * Q_BLOCK + jnp.arange(Q_BLOCK, dtype=jnp.int32)[None, :]
    k_pos = blk * Q_BLOCK - Q_BLOCK + jnp.arange(2 * Q_BLOCK, dtype=jnp.int32)[None, :]
    dist_i = q_pos[:, :, None] - k_pos[:, None, :]
    mask = (dist_i >= 0) & (dist_i < WINDOW) & (k_pos[:, None, :] >= 0)
    slopes = alibi_slopes(SWA_Q_HEADS).reshape(SWA_KV_HEADS, SWA_GROUP)
    bias = -slopes[None, :, :, None, None] * dist_i.astype(jnp.float32)[:, None, None]
    s = jnp.where(mask[None, :, None, None], s + bias[None], NEG_INF)
    sink = jnp.broadcast_to(sinks.astype(jnp.float32).reshape(1, 1, SWA_KV_HEADS, SWA_GROUP, 1, 1),
                            s.shape[:-1] + (1,))
    p = jax.nn.softmax(jnp.concatenate([s, sink], axis=-1), axis=-1)[..., :-1]
    o = jnp.einsum('bnkgqs,bnskd->bnqkgd', p.astype(vv.dtype), vv)
    return o.reshape(B, S, SWA_WIDTH)

def setup_inputs(seed: int = 0) -> dict:
    key = jax.random.key(seed)
    ks = jax.random.split(key, 20)
    f32 = jnp.float32

    def w(k, shape, fan_in):
        return jax.random.normal(k, shape, f32) * (fan_in ** -0.5)

    def gain(k, dim):
        return 1.0 + 0.02 * jax.random.normal(k, (DEPTH, dim), f32)

    return {
        "x": jax.random.normal(ks[0], (BATCH, SEQ, D_MODEL), f32),
        "ffn1_norm_pre": gain(ks[1], D_MODEL),
        "ffn1_w_in": w(ks[2], (DEPTH, D_MODEL, 2 * D_FF), D_MODEL),
        "ffn1_w_out": w(ks[3], (DEPTH, D_FF, D_MODEL), D_FF),
        "ffn1_norm_post": gain(ks[4], D_MODEL),
        "mix_norm_pre": gain(ks[5], D_MODEL),
        "w_in": w(ks[6], (DEPTH, D_MODEL, IN_COLS), D_MODEL),
        "diff_lambda": 0.1 * jax.random.normal(ks[7], (DEPTH, 4, DIFF_HEAD_DIM), f32),
        "diff_subln": gain(ks[8], DIFF_V_DIM),
        "swa_sinks": 0.5 * jax.random.normal(ks[9], (DEPTH, SWA_Q_HEADS), f32),
        "w_branch_diff": w(ks[10], (DEPTH, DIFF_WIDTH, D_MODEL), DIFF_WIDTH),
        "w_branch_swa": w(ks[11], (DEPTH, SWA_WIDTH, D_MODEL), SWA_WIDTH),
        "w_out": w(ks[12], (DEPTH, D_MODEL, D_MODEL), D_MODEL),
        "mix_norm_post": gain(ks[13], D_MODEL),
        "ffn2_norm_pre": gain(ks[14], D_MODEL),
        "ffn2_w_in": w(ks[15], (DEPTH, D_MODEL, 2 * D_FF), D_MODEL),
        "ffn2_w_out": w(ks[16], (DEPTH, D_FF, D_MODEL), D_FF),
        "ffn2_norm_post": gain(ks[17], D_MODEL),
    }

def reference(x, ffn1_norm_pre, ffn1_w_in, ffn1_w_out, ffn1_norm_post, mix_norm_pre, w_in,
              diff_lambda, diff_subln, swa_sinks, w_branch_diff, w_branch_swa, w_out,
              mix_norm_post, ffn2_norm_pre, ffn2_w_in, ffn2_w_out, ffn2_norm_post):
    split_idx = []
    acc = 0
    for c in COL_SIZES[:-1]:
        acc += c
        split_idx.append(acc)
    for l in range(DEPTH):
        lam_init = 0.8 - 0.6 * math.exp(-0.3 * l)
        h = rmsnorm(x, ffn1_norm_pre[l])
        x = x + 0.5 * rmsnorm(swiglu(h, ffn1_w_in[l], ffn1_w_out[l]), ffn1_norm_post[l])
        h = rmsnorm(x, mix_norm_pre[l])
        proj = h @ w_in[l]
        dq, dk, dv, sq, sk, sv, gates = jnp.split(proj, split_idx, axis=-1)
        B, S = x.shape[0], x.shape[1]
        sk = sk.reshape(B, S, SWA_KV_HEADS, SWA_HEAD_DIM)
        sv = sv.reshape(B, S, SWA_KV_HEADS, SWA_HEAD_DIM)
        ya = diff_attention(dq, dk, dv, diff_lambda[l], diff_subln[l], lam_init) @ w_branch_diff[l]
        yb = swa_attention(sq, sk, sv, swa_sinks[l]) @ w_branch_swa[l]
        ga, gb = jnp.split(gates, 2, axis=-1)
        y = (jax.nn.sigmoid(ga) * ya + jax.nn.sigmoid(gb) * yb) @ w_out[l]
        x = x + rmsnorm(y, mix_norm_post[l])
        h = rmsnorm(x, ffn2_norm_pre[l])
        x = x + 0.5 * rmsnorm(swiglu(h, ffn2_w_in[l], ffn2_w_out[l]), ffn2_norm_post[l])
    return x


_drawn_inputs = setup_inputs


def setup_inputs(seed=0):
    import zlib

    import numpy as np

    out = dict(_drawn_inputs(seed))
    spreads = {}
    factors = {'ffn1_norm_pre': 3.036,
     'ffn1_norm_post': 4.606,
     'diff_subln': 11.218,
     'swa_sinks': 17.708,
     'mix_norm_post': 10.917,
     'ffn2_norm_pre': 18.579,
     'ffn2_norm_post': 117.278}
    for name, (base, spread) in spreads.items():
        noise = np.random.default_rng([zlib.crc32(name.encode()), seed]).standard_normal(out[name].shape)
        drawn = base * np.exp(spread * noise) if base else spread * noise
        out[name] = __import__('jax').numpy.asarray(drawn.astype(out[name].dtype))
    for name, factor in factors.items():
        out[name] = (out[name] * factor).astype(out[name].dtype)
    return out
```

```python
from contextlib import ExitStack

import numpy as np

import concourse.bass as bass
from concourse import mybir

F32 = mybir.dt.float32
F32R = mybir.dt.float32r
BF16 = mybir.dt.bfloat16
ALU = mybir.AluOpType
ACT = mybir.ActivationFunctionType
AX = mybir.AxisListType

P = 128
CW = 512
D_MODEL, SEQ, D_FF = 2048, 256, 5504
MT = SEQ // P
KT = D_MODEL // P
FT = D_FF // P
HEADS, HD = 8, 64
SWA_HEADS, KV_HEADS = 16, 4
WIDTH = 1024
WINDOW = 128
EPS = 1e-6
LAM_INIT = 0.8 - 0.6 * 1.0
MASKED = 1e34

SUBS = 8
NG = D_MODEL // CW
PAIRS = D_FF // CW
TAIL = D_FF - PAIRS * CW
OUT_GROUPS = [4] * 7 + [3] * 5
assert sum(OUT_GROUPS) == FT
QKV_LOOPS, QKV_CHUNKS, GATE_CHUNKS = 3, 9, 8
UNITS = 16
LEAD = 3

A8 = 0
B8 = A8 + 2 * (PAIRS + 1)
C8 = B8 + NG * 3
G8 = C8 + QKV_CHUNKS
D8 = G8 + GATE_CHUNKS
E8 = D8 + NG
F8 = E8 + NG
H8 = F8 + 2 * (PAIRS + 1)
TOTAL_SUBS = 8 * (H8 + NG * 3)

PC_START = 0
PC_A = PC_START + 8
PC_BC = PC_A + 2 * (PAIRS + 1)
PC_QK = PC_BC + 8
PC_SK = PC_QK + 12
PC_O = PC_SK + 2
PC_D = PC_O + 8
PC_EF = PC_D + 2 * NG
PC_F = PC_EF + 8
NO_SPLIT = 14
SC_START, SC_BC, SC_O, SC_EF = 0, 8, 16, 20
U_B = PAIRS + 1
U_C = U_B + 2
U_G = [U_C + 5, U_C + 4]
U_D = [U_C + 9, U_C + 8]
U_E = [U_D[0] + NG, U_D[1] + NG]
U_F = [U_E[0] + 2, U_E[1] + 2]
U_H = [U_F[0] + PAIRS + 1, U_F[1] + PAIRS + 1]
R_PRE = [0, 2, 12]
R_POST = [1, 11, 13]
R_HEAD = 3
ROOTS = 14
Q_X, Q_Y, Q_O = [0, 16, 48], [8, 40, 56], 24
FULL_SUBS = [[2 * j, 2 * j + 1] for j in range(SUBS)]


def out_subs():
    subs, k = [], 0
    for n in OUT_GROUPS:
        subs += [list(range(k, k + 2)), list(range(k + 2, k + n))]
        k += n
    return subs


HIDDEN_SUBS = out_subs()


def head_slope(n, i):
    return float(2.0 ** (-8.0 * (i + 1) / n))


def layer_kernel(nc, x, ffn1_norm_pre, ffn1_w_in, ffn1_w_out, ffn1_norm_post, mix_norm_pre, w_in,
                 diff_lambda, diff_subln, swa_sinks, w_branch_diff, w_branch_swa, w_out,
                 mix_norm_post, ffn2_norm_pre, ffn2_w_in, ffn2_w_out, ffn2_norm_post, out):
    with ExitStack() as ctx:
        base = (nc.sbuf_base + 31) // 32 * 32
        place = [base]

        def region(words):
            at = place[0]
            place[0] += 4 * words
            return at

        def sb(name, shape, dt, at):
            return nc.alloc_sbuf_tensor_at(name, shape, dt, offset=at)

        HALF = KT * P
        r_x = region(MT * D_MODEL)
        r_h = region(4 * HALF)
        r_act = region(2 * FT * SEQ)
        r_raw = region(4 * 4 * CW)
        r_hi = region(4 * 2 * CW)
        r_lo = region(4 * 2 * CW)
        r_stage = region(MT * CW)
        xs = sb("xs", [P, MT, D_MODEL], F32, r_x)
        h_hi = [sb(f"h_hi{m}", [P, KT, P], F32R, r_h + 8 * m * HALF) for m in range(MT)]
        h_lo = [sb(f"h_lo{m}", [P, KT, P], F32R, r_h + 8 * m * HALF + 4 * HALF) for m in range(MT)]
        y = [sb(f"y{m}", [P, D_MODEL], F32, r_h + 8 * m * HALF) for m in range(MT)]
        gain = sb("gain", [P, D_MODEL], F32, r_h + 12 * HALF)
        a_hi = sb("a_hi", [P, FT, SEQ], F32R, r_act)
        a_lo = sb("a_lo", [P, FT, SEQ], F32R, r_act + 4 * FT * SEQ)
        at = r_act
        qk = sb("qk", [P, 24, SEQ], F32, at)
        skt = sb("skt", [P, KV_HEADS, SEQ], F32, at + 4 * 24 * SEQ)
        dv = sb("dv", [P, MT, WIDTH], F32, at + 4 * 28 * SEQ)
        sv = sb("sv", [P, MT, KV_HEADS * HD], F32, at + 4 * 36 * SEQ)
        gates = sb("gates", [P, MT, 2 * D_MODEL], F32, at + 4 * 38 * SEQ)
        sc = sb("sc", [P, 2, 2, 3 * P], F32, at + 4 * 70 * SEQ)
        pt = sb("pt", [P, 2, 2, 3 * P], F32, at + 4 * 76 * SEQ)
        assert 82 * SEQ <= 2 * FT * SEQ
        z_hi = sb("z_hi", [P, KT, SEQ], F32R, at)
        z_lo = sb("z_lo", [P, KT, SEQ], F32R, at + 4 * KT * SEQ)
        raw = sb("raw", [P, 4, 4, CW], F32, r_raw)
        w_hi = sb("w_hi", [P, 4, 2, CW], F32R, r_hi)
        w_lo = sb("w_lo", [P, 4, 2, CW], F32R, r_lo)
        stage = sb("stage", [P, MT, CW], F32, r_stage)
        ident = sb("ident", [P, P], F32, region(P))
        dist = sb("dist", [P, 2, 3 * P], F32, region(6 * P))
        junk = sb("junk", [P, CW], BF16, region(CW // 2))
        rows = sb("rows", [P, P], F32, r_act)
        cols = sb("cols", [P, 3 * KT + 1], F32, region(56))
        lamp = sb("lamp", [P, 4, HD], F32, r_act + 4 * P)
        lprod = sb("lprod", [P, 2, HD], F32, r_act + 4 * P + 16 * HD)
        lsum = sb("lsum", [P, 2], F32, region(8))
        lexp = sb("lexp", [P, 2], F32, region(8))
        nlam = sb("nlam", [P, 1], F32, region(8))
        headgain = sb("headgain", [P, 1], F32, region(8))
        sink = sb("sink", [P, SWA_HEADS], F32, region(16))
        nsink = sb("nsink", [P, SWA_HEADS], F32, region(16))
        half = sb("half", [P, 2], F32, region(8))
        ssum = sb("ssum", [P, 2], F32, region(8))
        ssq = sb("ssq", [P, MT, NG], F32, region(8))
        ssx = sb("ssx", [P, MT, NG], F32, region(8))
        sso = sb("sso", [P, HEADS, MT], F32, region(16))
        var = sb("var", [P, ROOTS, MT], F32, region(32))
        root = sb("root", [P, ROOTS, MT], F32, region(32))
        qk_factor = sb("qk_factor", [P, QKV_LOOPS], F32, region(8))
        ssp = sb("ssp", [P, MT, 2], F32, region(8))
        nmax = sb("nmax", [P, 2, MT, 2], F32, region(8))
        tsink = sb("tsink", [P, 2, MT, 2], F32, region(8))
        esink = sb("esink", [P, 2, MT, 2], F32, region(8))
        sums = sb("sums", [P, 2, MT, 2], F32, region(8))
        rsum = sb("rsum", [P, 2, MT, 2], F32, region(8))
        mixw = sb("mixw", [P, 2, MT], F32, region(8))
        assert place[0] <= nc.sbuf_usable_end
        ctx.enter_context(nc.sbuf_tensor("arena", [P, (place[0] - base) // 4], F32))

        acc = ctx.enter_context(nc.psum_tensor("acc", [P, 2, MT, CW], F32))
        tp = ctx.enter_context(nc.psum_tensor("tp", [P, 4, CW], F32))

        def sem(name):
            return ctx.enter_context(nc.semaphore(name))

        x_in = [sem(f"x_in{q}") for q in range(NG)]
        small_in = sem("small_in")
        gain_in = sem("gain_in")
        raw_in = [sem(f"raw_in{s}") for s in range(4)]
        out_written = sem("out_written")
        consts_made = sem("consts_made")
        gp_step = sem("gp_step")
        hi_ready = sem("hi_ready")
        lo_ready = sem("lo_ready")
        multiplied = sem("multiplied")
        acc_free = [sem("acc_free0"), sem("acc_free1")]
        turned = sem("turned")
        scaled = sem("scaled")
        piece_hi = sem("piece_hi")
        piece_out = sem("piece_out")
        squared = sem("squared")
        x_new = sem("x_new")
        var_ready = sem("var_ready")
        root_ready = sem("root_ready")
        cols_turned = sem("cols_turned")
        cols_copied = sem("cols_copied")
        lam_sums = sem("lam_sums")
        lam_exps = sem("lam_exps")
        sig_ready = sem("sig_ready")
        z_ready = sem("z_ready")
        scored = sem("scored")
        score_read = sem("score_read")
        nmax_ready = sem("nmax_ready")
        exp_ready = sem("exp_ready")
        mixed = sem("mixed")
        p_turned = sem("p_turned")
        p_copied = sem("p_copied")
        pv_done = sem("pv_done")
        o_read = sem("o_read")
        o_scaled = sem("o_scaled")
        dve_step = sem("dve_step")

        def bank(q, m):
            return (2 * q + m + 2) % 4

        w1_in, w1_out = ffn1_w_in[0], ffn1_w_out[0]
        w2_in, w2_out = ffn2_w_in[0], ffn2_w_out[0]
        x_d = x[0].rearrange("(m p) n -> p m n", p=P)
        out_d = out[0].rearrange("(m p) n -> p m n", p=P)
        block = ctx.enter_context(nc.Block())

        @block.sync
        def _(sp):
            def load(b8, j, w, row, tiles, col, width):
                if not (isinstance(b8, int) and 4 * b8 + j < 4):
                    sp.wait_ge(lo_ready, b8 * 8 + (2 * j - 6))
                src = w[row:row + tiles * P, bass.ds(col, width)].rearrange("(k p) n -> p k n", p=P)
                sp.dma_start(raw[:, j % 4, 0:tiles, 0:width], src).then_inc(raw_in[j % 4], 16)

            def chunk(b8, w, col, width=CW):
                for j in range(4):
                    load(b8, j, w, j * 4 * P, 4, col, width)

            def gate_up(b8, w):
                def pair(i, width):
                    chunk(b8 + 2 * i, w, i * CW, width)
                    chunk(b8 + 2 * i + 1, w, D_FF + i * CW, width)
                pair(0, CW)
                with sp.Fori(1, PAIRS) as i:
                    pair(i, CW)
                pair(PAIRS, TAIL)

            def hidden_out(b8, w):
                with sp.Fori(0, NG) as n:
                    row = 0
                    for j, tiles in enumerate(OUT_GROUPS):
                        load(b8 + 3 * n, j, w, row * P, tiles, n * CW, CW)
                        row += tiles

            for q in range(NG):
                sp.dma_start(xs[:, :, q * CW:(q + 1) * CW], x_d[:, :, q * CW:(q + 1) * CW]).then_inc(x_in[q], 16)
            gate_up(A8, w1_in)
            hidden_out(B8, w1_out)
            dv_col, sq_col = 2 * WIDTH, 3 * WIDTH
            with sp.Fori(0, 2) as i:
                for h in range(2):
                    chunk(C8 + 2 * i + h, w_in[0], i * WIDTH + h * CW)
            for c, col in enumerate([sq_col, sq_col + CW, dv_col, dv_col + CW]):
                chunk(C8 + 4 + c, w_in[0], col)
            with sp.Fori(0, 1 + GATE_CHUNKS) as c:
                chunk(C8 + 8 + c, w_in[0], c * CW + 4 * WIDTH)
            with sp.Fori(0, NG) as n:
                for j in range(4):
                    w = (w_branch_diff, w_branch_swa)[j // 2][0]
                    load(D8 + n, j, w, j % 2 * 4 * P, 4, n * CW, CW)
            with sp.Fori(0, NG) as n:
                chunk(E8 + n, w_out[0], n * CW)
            gate_up(F8, w2_in)
            hidden_out(H8, w2_out)
            for q in range(NG):
                sp.wait_ge(x_new, 4 * 2 * 2 + 2 * (q + 1))
                sp.dma_start(out_d[:, :, q * CW:(q + 1) * CW], xs[:, :, q * CW:(q + 1) * CW]).then_inc(out_written, 16)
            sp.wait_ge(out_written, 16 * NG)

        @block.gpsimd
        def _(gp):
            steps = [0]

            def link(ins):
                steps[0] += 1
                ins.then_inc(gp_step, 1)
                gp.wait_ge(gp_step, steps[0])

            link(nc.gpsimd.memset(ident[:], 0.0))
            nc.gpsimd.affine_select(out=ident[:], in_=ident[:], compare_op=ALU.not_equal, fill=1.0, base=0,
                                    pattern=[[-1, P]], channel_multiplier=1).then_inc(consts_made, 1)
            nc.gpsimd.memset(half[:], -0.5).then_inc(consts_made, 1)
            for kind in range(2):
                nc.gpsimd.iota(dist[:, kind, 0:P], pattern=[[-1, P]], base=0, channel_multiplier=1,
                               allow_small_or_imprecise_dtypes=True)
                link(nc.gpsimd.iota(dist[:, kind, P:3 * P], pattern=[[-1, 2 * P]], base=P, channel_multiplier=1,
                                    allow_small_or_imprecise_dtypes=True))
                for lo, n, b in ((0, P, 0), (P, 2 * P, P)):
                    d = dist[:, kind, lo:lo + n]
                    link(nc.gpsimd.affine_select(out=d, in_=d, compare_op=ALU.is_ge, fill=MASKED, base=b,
                                                 pattern=[[-1, n]], channel_multiplier=1))
                    if kind:
                        link(nc.gpsimd.affine_select(out=d, in_=d, compare_op=ALU.is_ge, fill=MASKED,
                                                     base=WINDOW - 1 - b, pattern=[[1, n]],
                                                     channel_multiplier=-1))
            for n in range(ROOTS):
                gp.wait_ge(var_ready, n + 1)
                if n == 0:
                    gp.wait_ge(consts_made, 2)
                nc.gpsimd.tensor_tensor(root[:, n, :], var[:, n, :], half[:], ALU.pow).then_inc(root_ready, 1)

        @block.tensor
        def _(pe):
            def chunk(b8, par, lhs, subs, width=CW, before=None, at=0):
                for j, tiles in enumerate(subs):
                    if before and j in before:
                        before[j]()
                    s = at + j
                    pe.wait_ge(lo_ready, b8 * 8 + (s + 1))
                    for t, k in enumerate(tiles):
                        first = j == 0 and t == 0
                        last = j == len(subs) - 1 and t == len(tiles) - 1
                        wh, wl = w_hi[:, s % 4, t, 0:width], w_lo[:, s % 4, t, 0:width]
                        for m in range(MT):
                            xh, xl = lhs(k, m)
                            o = acc[:, par, m, 0:width]
                            nc.tensor.matmul(o, xh, wh, start=first, stop=False)
                            nc.tensor.matmul(o, xh, wl, start=False, stop=False)
                            mm = nc.tensor.matmul(o, xl, wh, start=False, stop=last)
                    mm.then_inc(multiplied, 1)

            def from_h(k, m):
                return h_hi[m][:, k, :], h_lo[m][:, k, :]

            def from_a(k, m):
                return a_hi[:, k, m * P:(m + 1) * P], a_lo[:, k, m * P:(m + 1) * P]

            def from_z(k, m):
                return z_hi[:, k, m * P:(m + 1) * P], z_lo[:, k, m * P:(m + 1) * P]

            def turn(src, b, tiles):
                for t in range(tiles):
                    mm = nc.tensor.transpose(tp[:, b, t * P:(t + 1) * P], src(t), ident[:])
                mm.then_inc(turned, 1)

            def turn_stage(pieces, tiles=4):
                pe.wait_ge(piece_out, pieces)
                for m in range(MT):
                    turn(lambda t: stage[:, m, t * P:(t + 1) * P], m, tiles)

            def boundary(pc, ready, src):
                def quarter(q):
                    for m in range(MT):
                        ready(q, m)
                        if pc + 2 * q + m - 4 >= 0 and q >= 2:
                            pe.wait_ge(piece_out, pc + 2 * q + m - 3)
                        elif q < 2 and pc:
                            pe.wait_ge(piece_out, pc)
                        turn(lambda t: src(4 * q + t, m), bank(q, m), 4)

                def have(q):
                    pe.wait_ge(piece_out, pc + 2 * (q + 1))
                return {0: lambda: (quarter(0), quarter(1), have(0)), 2: lambda: (quarter(2), have(1)),
                        4: lambda: (quarter(3), have(2)), 6: lambda: have(3)}

            def x_tile(k, m):
                return xs[:, m, k * P:(k + 1) * P]

            def gate_up(b8, pc, uses, hooks):
                def pair(i, width, gate_hooks):
                    if not isinstance(i, int) or uses[0] + i > 0:
                        pe.wait_ge(acc_free[0], 2 * (uses[0] + i))
                    chunk(b8 + 2 * i, 0, from_h, FULL_SUBS, width, gate_hooks)
                    if not isinstance(i, int) or uses[1] + i > 0:
                        pe.wait_ge(acc_free[1], 2 * (uses[1] + i))
                    chunk(b8 + 2 * i + 1, 1, from_h, FULL_SUBS, width)

                def turn_last(i):
                    def hook():
                        pe.wait_ge(acc_free[1], 2 * (uses[1] + i))
                        turn_stage(pc + 2 * (i - 1))
                    return hook
                pair(0, CW, hooks)
                with pe.Fori(1, PAIRS) as i:
                    pair(i, CW, {1: turn_last(i)})
                pair(PAIRS, TAIL, {1: turn_last(PAIRS)})
                pe.wait_ge(acc_free[1], 2 * (uses[1] + PAIRS + 1))
                turn_stage(pc + 2 * PAIRS, TAIL // P)

            def down(b8, uses, lhs, subs, pieces):
                late = {len(subs) - 3: lambda: pe.wait_ge(piece_out, pieces)}
                with pe.Fori(0, NG // 2) as t:
                    for par in range(2):
                        pe.wait_ge(acc_free[par], 2 * (uses[par] + t))
                        chunk(b8 + (2 * t + par) * (len(subs) // 8), par, lhs, subs, before=late)

            pe.wait_ge(small_in, 16 * 6)
            pe.wait_ge(consts_made, 1)
            nc.tensor.transpose(tp[:, 0, 0:3 * KT + 1], rows[0:3 * KT + 1, :],
                                ident[0:3 * KT + 1, 0:3 * KT + 1]).then_inc(cols_turned, 1)
            pe.wait_ge(cols_copied, 1)

            gate_up(A8, PC_A, [0, 0],
                    boundary(PC_START, lambda q, m: pe.wait_ge(x_in[q], 16), x_tile))
            down(B8, [U_B, U_B], from_a, HIDDEN_SUBS, PC_BC)

            def turn_qk(c, par, i):
                def hook():
                    pe.wait_ge(acc_free[par], 2 * (U_C + i + 1))
                    turn_stage(PC_QK + 2 * c)
                return hook

            def qk_pair(i, first_hooks):
                for par in range(2):
                    pe.wait_ge(acc_free[par], 2 * (U_C + i))
                    chunk(C8 + 2 * i + par, par, from_h, FULL_SUBS,
                          before={2: turn_qk(2 * i, 0, i)} if par else first_hooks)

            qk_pair(0, boundary(PC_BC, lambda q, m: pe.wait_ge(x_new, 2 * q + m + 1), x_tile))
            with pe.Fori(1, QKV_LOOPS) as i:
                qk_pair(i, {2: turn_qk(2 * i - 1, 1, i - 1)})
            for c in range(6, QKV_CHUNKS):
                pe.wait_ge(acc_free[c % 2], 2 * (U_C + c // 2))
                chunk(C8 + c, c % 2, from_h, FULL_SUBS, before={2: turn_qk(5, 1, 2)} if c == 6 else None)

            def scores(u):
                qt = u if u < HEADS else 16 + u - HEADS
                if u:
                    pe.wait_ge(score_read, u)
                if u == 0:
                    pe.wait_ge(piece_out, PC_SK)
                for c in range(2):
                    r = slice(c * HD, (c + 1) * HD)
                    kt = qk[r, HEADS + u, :] if u < HEADS else skt[r, (u - HEADS) // 2, :]
                    nc.tensor.matmul(tp[:, 2 + c, 0:P], qk[r, qt, 0:P], kt[:, 0:P], start=True, stop=True)
                    mm = nc.tensor.matmul(tp[:, 2 + c, P:3 * P], qk[r, qt, P:2 * P], kt, start=True, stop=True)
                mm.then_inc(scored, 1)

            def turn_p(u):
                pe.wait_ge(mixed, u + 1)
                if u:
                    pe.wait_ge(o_read, u)
                else:
                    pe.wait_ge(piece_out, PC_O)
                for c in range(1 if u < HEADS else 2):
                    for b in range(3):
                        mm = nc.tensor.transpose(tp[:, c, b * P:(b + 1) * P], sc[:, u % 2, c, b * P:(b + 1) * P],
                                                 ident[:])
                mm.then_inc(p_turned, 1)

            def pv(u):
                pe.wait_ge(p_copied, u + 1)
                for c in range(1 if u < HEADS else 2):
                    n = P if u < HEADS else HD
                    for m in range(MT):
                        o = tp[:, m, 3 * P + c * HD:3 * P + c * HD + n]
                        for k in range(m + 1):
                            v = dv[:, k, u * P:(u + 1) * P] if u < HEADS else \
                                sv[:, k, (u - HEADS) // 2 * HD:(u - HEADS) // 2 * HD + HD]
                            b = m + k
                            mm = nc.tensor.matmul(o, pt[:, u % 2, c, b * P:(b + 1) * P], v,
                                                  start=(k == 0), stop=(k == m))
                mm.then_inc(pv_done, 1)

            hooks = {}
            for u in range(UNITS):
                hooks.setdefault(4 * u, []).append(lambda u=u: scores(u))
                hooks.setdefault(4 * u + 3, []).append(lambda u=u: turn_p(u))
                hooks.setdefault(4 * u + 5, []).append(lambda u=u: pv(u))

            def turn_sk():
                pe.wait_ge(acc_free[0], 2 * (U_C + QKV_CHUNKS // 2 + 1))
                turn_stage(PC_SK)
            hooks[1] = [turn_sk]
            for g in range(GATE_CHUNKS):
                par = (QKV_CHUNKS + g) % 2
                pe.wait_ge(acc_free[par], 2 * (U_C + (QKV_CHUNKS + g) // 2))
                chunk(G8 + g, par, from_h, FULL_SUBS,
                      before={j: (lambda fs=hooks[8 * g + j]: [f() for f in fs])
                              for j in range(8) if 8 * g + j in hooks})

            def o_tile(k, m):
                return qk[:, k if k < HEADS else 16 + k - HEADS, m * P:(m + 1) * P]

            def o_ready(q, m):
                if q < 2:
                    pe.wait_ge(o_scaled, HEADS)
                    if q == 1:
                        pe.wait_ge(o_read, UNITS)
                else:
                    pe.wait_ge(o_read, UNITS)

            def branch(n, first, second):
                for par, hk in ((0, first), (1, second)):
                    pe.wait_ge(acc_free[par], 2 * (U_D[par] + n))
                    chunk(D8 + n, par, from_h, FULL_SUBS[4 * par:4 * par + 4], before=hk, at=4 * par)

            def turn_z(n):
                def hook():
                    pe.wait_ge(z_ready, 2 * n)
                    turn_stage(PC_D + 2 * (n - 1))
                return hook
            pv(UNITS - 1)
            hk = boundary(PC_O, o_ready, o_tile)
            branch(0, {0: hk[0], 2: hk[2]}, {0: hk[4], 2: hk[6]})
            with pe.Fori(1, NG) as n:
                branch(n, {1: turn_z(n)}, None)
            turn_z(NG)()

            down(E8, U_E, from_z, FULL_SUBS, PC_EF)
            gate_up(F8, PC_F, U_F,
                    boundary(PC_EF, lambda q, m: pe.wait_ge(x_new, 8 + 2 * q + m + 1), x_tile))
            down(H8, U_H, from_a, HIDDEN_SUBS, PC_F + 2 * (PAIRS + 1))

        @block.scalar
        def _(act):
            def split(b8, j):
                s = j + LEAD
                if isinstance(b8, int) and 8 * b8 + s >= TOTAL_SUBS:
                    return
                g = s // 2
                if s % 2 == 0 or (isinstance(b8, int) and 8 * b8 + s < 4 and s % 2 == 0):
                    act.wait_ge(raw_in[g % 4], b8 * 16 + 16 * (g // 4 + 1))
                if not (isinstance(b8, int) and 8 * b8 + s < 4):
                    act.wait_ge(multiplied, b8 * 8 + (s - 3))
                nc.scalar.activation(w_hi[:, s % 4], raw[:, g % 4, s % 2 * 2:s % 2 * 2 + 2], ACT.Copy)\
                    .then_inc(hi_ready, 1)

            def steps(b8, n, before=None):
                for j in range(n):
                    if before and j in before:
                        before[j]()
                    split(b8, j)

            def await_turned(pc):
                return lambda: act.wait_ge(turned, pc + 2)

            def plain_hi(dst, tiles=4):
                for m in range(MT):
                    nc.scalar.activation(dst(m), tp[:, m, 0:tiles * P], ACT.Copy).then_inc(piece_hi, 1)

            def boundary(sc0, pc=None):
                def quarter(q):
                    for m in range(MT):
                        if pc is not None and q >= 2:
                            act.wait_ge(turned, pc + 2 * q + m + 1)
                            src = tp[:, bank(q, m), :]
                        else:
                            act.wait_ge(scaled, sc0 + 2 * q + m + 1)
                            src = stage[:, m, :]
                        nc.scalar.activation(h_hi[m][:, 4 * q:4 * q + 4, :], src, ACT.Copy).then_inc(piece_hi, 1)
                return {0: lambda: quarter(0), 1: lambda: quarter(1), 3: lambda: quarter(2), 5: lambda: quarter(3)}

            def square(n, src, total):
                if not (isinstance(n, int) and n == 0):
                    act.wait_ge(squared, n)
                nc.scalar.activation(junk[:, 0:src.shape[-1]], src, ACT.Square, accum_out=total)\
                    .then_inc(squared, 1)

            def square_x(k):
                def hook():
                    for m in range(MT):
                        for q in range(NG):
                            if k == 0:
                                act.wait_ge(x_in[q], 16)
                            square(Q_X[k] + m * NG + q, xs[:, m, q * CW:(q + 1) * CW], ssx[:, m, q:q + 1])
                return hook

            def gate_up(b8, pc, uses, k, hooks):
                def pair(i, width, gate_hooks):
                    steps(b8 + 2 * i, 8, gate_hooks)
                    if isinstance(i, int) and i == 0:
                        act.wait_ge(root_ready, R_PRE[k] + 1)
                    act.wait_ge(turned, pc + 2 * i)
                    act.wait_ge(multiplied, (b8 + 2 * i) * 8 + 8)
                    for m in range(MT):
                        nc.scalar.activation(stage[:, m, 0:width], acc[:, 0, m, 0:width], ACT.Silu,
                                             scale=root[:, R_PRE[k], m:m + 1]).then_inc(acc_free[0], 1)
                    steps(b8 + 2 * i + 1, 8)

                def last_hi(i):
                    return {4: await_turned(pc + 2 * (i - 1)),
                            5: lambda: plain_hi(lambda m: a_hi[:, bass.ds(4 * (i - 1), 4), m * P:(m + 1) * P])}
                pair(0, CW, hooks)
                with act.Fori(1, PAIRS) as i:
                    pair(i, CW, last_hi(i))
                pair(PAIRS, TAIL, last_hi(PAIRS))
                n = TAIL // P
                await_turned(pc + 2 * PAIRS)()
                plain_hi(lambda m: a_hi[:, 4 * PAIRS:4 * PAIRS + n, m * P:(m + 1) * P], n)

            def down(b8, units, k, g_d, last):
                act.wait_ge(multiplied, 8 * b8)
                act.dma_start(gain[:], g_d[0:1, :].partition_broadcast(P)).then_inc(gain_in, 16)

                def two(t):
                    for par in range(2):
                        n8 = b8 + (2 * t + par) * units
                        steps(n8, 8 * units)
                        act.wait_ge(multiplied, (n8 + units) * 8)
                        for m in range(MT):
                            square((2 * t + par) * 2 + (Q_Y[k] + m), acc[:, par, m, :], ssp[:, m, par:par + 1])
                if last:
                    two(0)
                    two(1)
                else:
                    with act.Fori(0, NG // 2) as t:
                        two(t)

            for k, g in enumerate((ffn1_norm_pre, mix_norm_pre, ffn2_norm_pre)):
                act.dma_start(rows[k * KT:(k + 1) * KT, :], g[0].rearrange("(t p) -> t p", p=P)).then_inc(small_in, 16)
            act.dma_start(rows[3 * KT:3 * KT + 1, :], diff_subln[0:1, :]).then_inc(small_in, 16)
            act.dma_start(lamp[:], diff_lambda.rearrange("a b c -> a (b c)").partition_broadcast(P)).then_inc(small_in, 16)
            act.dma_start(sink[:], swa_sinks[0:1, :].partition_broadcast(P)).then_inc(small_in, 16)
            act.wait_ge(lam_sums, 1)
            nc.scalar.activation(lexp[:], lsum[:], ACT.Exp).then_inc(lam_exps, 1)
            for j in range(-LEAD, 0):
                split(0, j)

            hooks = boundary(SC_START)
            hooks[6] = square_x(0)
            gate_up(A8, PC_A, [0, 0], 0, hooks)
            down(B8, 3, 0, ffn1_norm_post, False)

            def to_stage(par, c):
                act.wait_ge(turned, PC_QK + 2 * c)
                act.wait_ge(multiplied, (C8 + c) * 8 + 8)
                for m in range(MT):
                    nc.scalar.activation(stage[:, m, :], acc[:, par, m, :], ACT.Copy,
                                         scale=root[:, R_PRE[1], m:m + 1]).then_inc(acc_free[par], 1)

            def qk_pair(i, hooks):
                for par in range(2):
                    steps(C8 + 2 * i + par, 8, None if par else hooks)
                    if isinstance(i, int) and i == 0 and par == 0:
                        act.wait_ge(root_ready, R_PRE[1] + 1)
                    to_stage(par, 2 * i + par)
            hooks = boundary(SC_BC)
            hooks[6] = square_x(1)
            qk_pair(0, hooks)
            with act.Fori(1, QKV_LOOPS) as i:
                qk_pair(i, None)
            rs = R_PRE[1]
            for c in (6, 7):
                steps(C8 + c, 8)
                act.wait_ge(multiplied, (C8 + c) * 8 + 8)
                for m in range(MT):
                    nc.scalar.activation(dv[:, m, (c - 6) * CW:(c - 5) * CW], acc[:, c % 2, m, :], ACT.Copy,
                                         scale=root[:, rs, m:m + 1]).then_inc(acc_free[c % 2], 1)
            steps(C8 + 8, 8)
            act.wait_ge(turned, PC_SK)
            act.wait_ge(multiplied, (C8 + 8) * 8 + 8)
            KW = KV_HEADS * HD
            for m in range(MT):
                dup = stage[:, m, :].rearrange("p (h two d) -> p h two d", two=2, d=HD)
                for two in range(2):
                    nc.scalar.activation(dup[:, :, two, :], acc[:, 0, m, 0:KW].rearrange("p (h d) -> p h d", d=HD),
                                         ACT.Copy, scale=root[:, rs, m:m + 1])
                nc.scalar.activation(sv[:, m, :], acc[:, 0, m, KW:2 * KW], ACT.Copy,
                                     scale=root[:, rs, m:m + 1]).then_inc(acc_free[0], 1)

            def exps(u):
                act.wait_ge(nmax_ready, u + 1)
                b = u % 2
                for c in range(2):
                    for m in range(MT):
                        s = sc[:, b, c, m * P:P + 2 * m * P]
                        ins = nc.scalar.activation(s, s, ACT.Exp, bias=nmax[:, b, m, c:c + 1],
                                                   accum_out=sums[:, b, m, c:c + 1])
                if u >= HEADS:
                    ins = nc.scalar.activation(esink[:, b], tsink[:, b], ACT.Exp)
                ins.then_inc(exp_ready, 1)

            def copy_p(u):
                act.wait_ge(p_turned, u + 1)
                if u >= 2:
                    act.wait_ge(pv_done, u - 1)
                n = 1 if u < HEADS else 2
                nc.scalar.activation(pt[:, u % 2, 0:n], tp[:, 0:n, 0:3 * P], ACT.Copy).then_inc(p_copied, 1)

            def square_o(u):
                act.wait_ge(o_read, u + 1)
                for m in range(MT):
                    square(Q_O + 2 * u + m, qk[:, u, m * P:(m + 1) * P], sso[:, u, m:m + 1])

            hooks = {}
            for u in range(UNITS):
                hooks.setdefault(4 * u + 1, []).append(lambda u=u: exps(u))
                hooks.setdefault(4 * u + 4, []).append(lambda u=u: copy_p(u))
                if u < HEADS:
                    hooks.setdefault(4 * u + 7, []).append(lambda u=u: square_o(u))
            for g in range(GATE_CHUNKS):
                par = (QKV_CHUNKS + g) % 2
                steps(G8 + g, 8, {j: (lambda fs=hooks[8 * g + j]: [f() for f in fs])
                                  for j in range(8) if 8 * g + j in hooks})
                act.wait_ge(multiplied, (G8 + g) * 8 + 8)
                for m in range(MT):
                    nc.scalar.activation(gates[:, m, g * CW:(g + 1) * CW], acc[:, par, m, :], ACT.Copy,
                                         scale=root[:, rs, m:m + 1]).then_inc(acc_free[par], 1)
            copy_p(UNITS - 1)

            def sigmoids(n):
                def hook():
                    for m in range(MT):
                        for side in range(2):
                            g = gates[:, m, bass.ds(side * D_MODEL + n * CW, CW)]
                            nc.scalar.activation(g, g, ACT.Sigmoid).then_inc(sig_ready, 1)
                return hook

            def z_piece_hi(n):
                plain_hi(lambda m: z_hi[:, bass.ds(4 * (n - 1), 4), m * P:(m + 1) * P])
            hooks = boundary(SC_O, PC_O)
            hooks[7] = sigmoids(0)
            act.wait_ge(acc_free[0], 2 * U_D[0])
            act.wait_ge(acc_free[1], 2 * U_D[1])
            act.wait_ge(multiplied, 8 * D8)
            steps(D8, 8, hooks)
            with act.Fori(1, NG) as n:
                steps(D8 + n, 8, {2: sigmoids(n), 4: await_turned(PC_D + 2 * (n - 1)),
                                  5: lambda: z_piece_hi(n)})
            await_turned(PC_D + 2 * (NG - 1))()
            z_piece_hi(NG)

            down(E8, 1, 1, mix_norm_post, False)
            hooks = boundary(SC_EF)
            hooks[6] = square_x(2)
            gate_up(F8, PC_F, U_F, 2, hooks)
            down(H8, 3, 2, ffn2_norm_post, True)

        @block.vector
        def _(dve):
            chain = [0]

            def link(ins):
                chain[0] += 1
                ins.then_inc(dve_step, 1)
                dve.wait_ge(dve_step, chain[0])

            def split(b8, j):
                s = j + LEAD
                if isinstance(b8, int) and 8 * b8 + s >= TOTAL_SUBS:
                    return
                g = s // 2
                dve.wait_ge(hi_ready, b8 * 8 + (s + 1))
                nc.vector.tensor_tensor(w_lo[:, s % 4], raw[:, g % 4, s % 2 * 2:s % 2 * 2 + 2],
                                        w_hi[:, s % 4].bitcast(F32), ALU.subtract).then_inc(lo_ready, 1)

            def steps(b8, n, before=None):
                for j in range(n):
                    if before and j in before:
                        before[j]()
                    split(b8, j)

            def plain_lo(pc, skip, hi, lo, tiles=4):
                for m in range(MT):
                    dve.wait_ge(piece_hi, pc - skip + m + 1)
                    nc.vector.tensor_tensor(lo(m), tp[:, m, 0:tiles * P].rearrange("p (t n) -> p t n", n=P),
                                            hi(m).bitcast(F32), ALU.subtract).then_inc(piece_out, 1)

            def boundary(pc, skip, gains, update=None):
                def quarter(q):
                    for m in range(MT):
                        g = gains(q)
                        if g is None:
                            continue
                        dve.wait_ge(turned, pc + 2 * q + m + 1)
                        if q:
                            dve.wait_ge(piece_out, pc + 2 * q + m - 1)
                        nc.vector.tensor_tensor(stage[:, m, :].rearrange("p (t n) -> p t n", n=P),
                                                tp[:, bank(q, m), :].rearrange("p (t n) -> p t n", n=P), g,
                                                ALU.mult).then_inc(scaled, 1)
                    for m in range(MT):
                        dve.wait_ge(piece_hi, pc - skip + 2 * q + m + 1)
                        src = stage[:, m, :] if gains(q) is not None else tp[:, bank(q, m), :]
                        nc.vector.tensor_tensor(h_lo[m][:, 4 * q:4 * q + 4, :], src.rearrange("p (t n) -> p t n", n=P),
                                                h_hi[m][:, 4 * q:4 * q + 4, :].bitcast(F32),
                                                ALU.subtract).then_inc(piece_out, 1)

                def new_x(q):
                    if update:
                        update(q)
                return {0: lambda: (new_x(0), new_x(1), quarter(0)), 1: lambda: (new_x(2), quarter(1)),
                        3: lambda: (new_x(3), quarter(2)), 5: lambda: quarter(3)}

            def pre_gain(k):
                return lambda q: cols[:, k * KT + 4 * q:k * KT + 4 * q + 4].unsqueeze(2).to_broadcast([P, 4, P])

            def variance(n, total, width, factor=1.0):
                nc.vector.tensor_scalar(var[:, n, :], total, 1.0 / (width * factor ** 2), EPS / factor ** 2,
                                        ALU.mult, ALU.add).then_inc(var_ready, 1)

            def pre_norm(k):
                def hook():
                    dve.wait_ge(squared, Q_X[k] + 8)
                    link(nc.vector.tensor_reduce(ssum[:], ssx[:], AX.X, ALU.add))
                    variance(R_PRE[k], ssum[:], D_MODEL)
                return hook

            def post_norm(k, factor):
                dve.wait_ge(acc_free[1], 2 * (U_C, U_F[1], U_H[1] + 2)[k])
                link(nc.vector.tensor_reduce(ssum[:], ssq[:], AX.X, ALU.add))
                variance(R_POST[k], ssum[:], D_MODEL, factor)

                def update(q):
                    if q == 0:
                        dve.wait_ge(root_ready, R_POST[k] + 1)
                    for m in range(MT):
                        c = slice(q * CW, (q + 1) * CW)
                        nc.vector.scalar_tensor_tensor(out=xs[:, m, c], in0=y[m][:, c],
                                                       scalar=root[:, R_POST[k], m:m + 1], in1=xs[:, m, c],
                                                       op0=ALU.mult, op1=ALU.add).then_inc(x_new, 1)
                return update

            def gate_up(b8, pc, skip, uses, k, hooks):
                def pair(i, width, gate_hooks):
                    steps(b8 + 2 * i, 8, gate_hooks)
                    steps(b8 + 2 * i + 1, 8)
                    dve.wait_ge(multiplied, (b8 + 2 * i) * 8 + 16)
                    dve.wait_ge(acc_free[0], 2 * (uses[0] + i + 1))
                    for m in range(MT):
                        nc.vector.scalar_tensor_tensor(out=stage[:, m, 0:width], in0=acc[:, 1, m, 0:width],
                                                       scalar=root[:, R_PRE[k], m:m + 1],
                                                       in1=stage[:, m, 0:width],
                                                       op0=ALU.mult, op1=ALU.mult).then_inc(acc_free[1], 1)

                def last_lo(i):
                    return lambda: plain_lo(pc + 2 * (i - 1), skip,
                                            lambda m: a_hi[:, bass.ds(4 * (i - 1), 4), m * P:(m + 1) * P],
                                            lambda m: a_lo[:, bass.ds(4 * (i - 1), 4), m * P:(m + 1) * P])
                pair(0, CW, hooks)
                with dve.Fori(1, PAIRS) as i:
                    pair(i, CW, {4: last_lo(i)})
                pair(PAIRS, TAIL, {4: last_lo(PAIRS)})
                n = TAIL // P
                plain_lo(pc + 2 * PAIRS, skip, lambda m: a_hi[:, 4 * PAIRS:4 * PAIRS + n, m * P:(m + 1) * P],
                         lambda m: a_lo[:, 4 * PAIRS:4 * PAIRS + n, m * P:(m + 1) * P], n)

            def down(b8, units, k, last):
                def two(t):
                    for par in range(2):
                        n8 = b8 + (2 * t + par) * units
                        steps(n8, 8 * units)
                        dve.wait_ge(gain_in, 16 * (k + 1))
                        for m in range(MT):
                            dve.wait_ge(squared, (2 * t + par) * 2 + (Q_Y[k] + m + 1))
                            nc.vector.tensor_copy(ssq[:, m, bass.ds(2 * t + par, 1)], ssp[:, m, par:par + 1])
                            nc.vector.tensor_tensor(y[m][:, bass.ds((2 * t + par) * CW, CW)], acc[:, par, m, :],
                                                    gain[:, bass.ds((2 * t + par) * CW, CW)],
                                                    ALU.mult).then_inc(acc_free[par], 1)
                if last:
                    two(0)
                    two(1)
                else:
                    with dve.Fori(0, NG // 2) as t:
                        two(t)

            dve.wait_ge(small_in, 16 * 6)
            nc.vector.tensor_tensor(lprod[:, 0, :], lamp[:, 0, :], lamp[:, 1, :], ALU.mult)
            link(nc.vector.tensor_tensor(lprod[:, 1, :], lamp[:, 2, :], lamp[:, 3, :], ALU.mult))
            nc.vector.tensor_reduce(lsum[:], lprod[:], AX.X, ALU.add).then_inc(lam_sums, 1)
            nc.vector.tensor_scalar(nsink[:], sink[:], -1.0, None, ALU.mult)
            dve.wait_ge(cols_turned, 1)
            nc.vector.tensor_copy(cols[:], tp[:, 0, 0:3 * KT + 1]).then_inc(cols_copied, 1)
            dve.wait_ge(cols_copied, 1)
            nc.vector.tensor_scalar(headgain[:], cols[:, 3 * KT:3 * KT + 1], 1.0 - LAM_INIT, None, ALU.mult)
            dve.wait_ge(lam_exps, 1)
            link(nc.vector.tensor_tensor(nlam[:], lexp[:, 1:2], lexp[:, 0:1], ALU.subtract))
            link(nc.vector.tensor_scalar(nlam[:], nlam[:], -LAM_INIT, None, ALU.add))
            for j in range(-LEAD, 0):
                split(0, j)

            hooks = boundary(PC_START, 0, pre_gain(0))
            hooks[7] = pre_norm(0)
            gate_up(A8, PC_A, 0, [0, 0], 0, hooks)
            down(B8, 3, 0, False)

            hooks = boundary(PC_BC, 0, pre_gain(1), post_norm(0, 0.5))
            hooks[7] = pre_norm(1)

            for i in range(QKV_LOOPS):
                ins = nc.vector.memset(qk_factor[:, i:i + 1], 1.0 if i == 1 else HD ** -0.5)
            link(ins)

            def take_qk(c, i):
                def hook():
                    for m in range(MT):
                        dve.wait_ge(turned, PC_QK + 2 * c + m + 1)
                        nc.vector.tensor_scalar(qk[:, bass.ds(4 * c, 4), m * P:(m + 1) * P],
                                                tp[:, m, :].rearrange("p (t n) -> p t n", n=P),
                                                qk_factor[:, bass.ds(i, 1)], None, ALU.mult).then_inc(piece_out, 1)
                return hook

            def qk_pair(i, first_hooks):
                steps(C8 + 2 * i, 8, first_hooks)
                steps(C8 + 2 * i + 1, 8, {4: take_qk(2 * i, i)})
            qk_pair(0, hooks)
            with dve.Fori(1, QKV_LOOPS) as i:
                qk_pair(i, {4: take_qk(2 * i - 1, i - 1)})
            steps(C8 + 6, 8, {4: take_qk(5, 2)})
            steps(C8 + 7, 8)
            steps(C8 + 8, 8)

            def scores_read(u):
                b = u % 2
                dve.wait_ge(scored, u + 1)
                if u >= 2:
                    dve.wait_ge(p_turned, u - 1)
                if u < HEADS:
                    ins = nc.vector.scalar_tensor_tensor(
                        out=sc[:, b], in0=dist[:, 0:1, :].to_broadcast([P, 2, 3 * P]), scalar=-head_slope(HEADS, u),
                        in1=tp[:, 2:4, 0:3 * P], op0=ALU.mult, op1=ALU.add)
                else:
                    for c in range(2):
                        ins = nc.vector.scalar_tensor_tensor(
                            out=sc[:, b, c], in0=dist[:, 1, :],
                            scalar=-head_slope(SWA_HEADS, 2 * (u - HEADS) + c),
                            in1=tp[:, 2 + c, 0:3 * P], op0=ALU.mult, op1=ALU.add)
                ins.then_inc(score_read, 1)
                dve.wait_ge(score_read, u + 1)
                for m in range(MT):
                    ins = nc.vector.tensor_reduce(nmax[:, b, m, :], sc[:, b, :, m * P:P + 2 * m * P], AX.X,
                                                  ALU.max, negate=True)
                if u >= HEADS:
                    link(ins)
                    h = 2 * (u - HEADS)
                    link(nc.vector.tensor_tensor(nmax[:, b], nmax[:, b],
                                                 nsink[:, h:h + 2].unsqueeze(1).to_broadcast([P, MT, 2]), ALU.min))
                    ins = nc.vector.tensor_tensor(tsink[:, b], nmax[:, b],
                                                  sink[:, h:h + 2].unsqueeze(1).to_broadcast([P, MT, 2]), ALU.add)
                ins.then_inc(nmax_ready, 1)

            def mix(u):
                b = u % 2
                dve.wait_ge(exp_ready, u + 1)
                if u < HEADS:
                    link(nc.vector.reciprocal(rsum[:, b], sums[:, b]))
                    link(nc.vector.scalar_tensor_tensor(out=mixw[:, b], in0=sums[:, b, :, 0], scalar=nlam[:],
                                                        in1=rsum[:, b, :, 1], op0=ALU.mult, op1=ALU.mult))
                    for m in range(MT):
                        r = slice(m * P, P + 2 * m * P)
                        ins = nc.vector.scalar_tensor_tensor(out=sc[:, b, 0, r], in0=sc[:, b, 1, r],
                                                             scalar=mixw[:, b, m:m + 1], in1=sc[:, b, 0, r],
                                                             op0=ALU.mult, op1=ALU.add)
                else:
                    link(nc.vector.tensor_tensor(sums[:, b], sums[:, b], esink[:, b], ALU.add))
                    ins = nc.vector.reciprocal(rsum[:, b], sums[:, b])
                ins.then_inc(mixed, 1)

            def take_o(u):
                b = u % 2
                dve.wait_ge(pv_done, u + 1)
                dve.wait_ge(mixed, u + 1)
                if u < HEADS:
                    ins = nc.vector.tensor_tensor(qk[:, u, :].rearrange("p (m n) -> p m n", n=P),
                                                  tp[:, 0:2, 3 * P:4 * P],
                                                  rsum[:, b, :, 0:1].to_broadcast([P, MT, P]), ALU.mult)
                else:
                    ins = nc.vector.tensor_tensor(
                        qk[:, 16 + u - HEADS, :].rearrange("p (m c n) -> p m c n", c=2, n=HD),
                        tp[:, 0:2, 3 * P:4 * P].rearrange("p m (c n) -> p m c n", n=HD),
                        rsum[:, b].unsqueeze(3).to_broadcast([P, MT, 2, HD]), ALU.mult)
                ins.then_inc(o_read, 1)

            def head_var(u):
                dve.wait_ge(squared, Q_O + 2 * u + 2)
                variance(R_HEAD + u, sso[:, u, :], 2 * HD)

            def head_scale(u):
                dve.wait_ge(root_ready, R_HEAD + u + 1)
                dve.wait_ge(o_read, u + 1)
                o = qk[:, u, :].rearrange("p (m n) -> p m n", n=P)
                nc.vector.tensor_tensor(o, o, root[:, R_HEAD + u, :].unsqueeze(2).to_broadcast([P, MT, P]),
                                        ALU.mult).then_inc(o_scaled, 1)

            def take_sk():
                for m in range(MT):
                    dve.wait_ge(turned, PC_SK + m + 1)
                    nc.vector.tensor_copy(skt[:, :, m * P:(m + 1) * P],
                                          tp[:, m, :].rearrange("p (t n) -> p t n", n=P)).then_inc(piece_out, 1)

            hooks = {}
            for u in range(UNITS):
                hooks.setdefault(4 * u + 1, []).append(lambda u=u: scores_read(u))
                hooks.setdefault(4 * u + 2, []).append(lambda u=u: mix(u))
                hooks.setdefault(4 * u + 6, []).append(lambda u=u: take_o(u))
                if u < HEADS:
                    hooks.setdefault(4 * u + 8, []).append(lambda u=u: head_var(u))
                    hooks.setdefault(4 * u + 11, []).append(lambda u=u: head_scale(u))
            hooks[2].insert(0, take_sk)
            for g in range(GATE_CHUNKS):
                steps(G8 + g, 8, {j: (lambda fs=hooks[8 * g + j]: [f() for f in fs])
                                  for j in range(8) if 8 * g + j in hooks})
            take_o(UNITS - 1)

            def head_gain(q):
                return headgain[:, 0:1].unsqueeze(2).to_broadcast([P, 4, P]) if q < 2 else None
            hooks = boundary(PC_O, NO_SPLIT, head_gain)

            def gate_side(side, n):
                dve.wait_ge(multiplied, (D8 + n) * 8 + 4 * (side + 1))
                dve.wait_ge(sig_ready, 4 * n + 4)
                for m in range(MT):
                    g = gates[:, m, bass.ds(side * D_MODEL + n * CW, CW)]
                    nc.vector.tensor_tensor(g, g, acc[:, side, m, :], ALU.mult).then_inc(acc_free[side], 1)

            def gate_sum(n):
                if not (isinstance(n, int) and n == 0):
                    dve.wait_ge(turned, PC_D + 2 * n)
                dve.wait_ge(acc_free[1], 2 * (U_D[1] + 1 + n))
                for m in range(MT):
                    nc.vector.tensor_tensor(stage[:, m, :], gates[:, m, bass.ds(n * CW, CW)],
                                            gates[:, m, bass.ds(D_MODEL + n * CW, CW)],
                                            ALU.add).then_inc(z_ready, 1)

            def z_piece_lo(n):
                plain_lo(PC_D + 2 * (n - 1), NO_SPLIT,
                         lambda m: z_hi[:, bass.ds(4 * (n - 1), 4), m * P:(m + 1) * P],
                         lambda m: z_lo[:, bass.ds(4 * (n - 1), 4), m * P:(m + 1) * P])
            steps(D8, 8, hooks)
            gate_side(0, 0)
            gate_side(1, 0)
            gate_sum(0)
            with dve.Fori(1, NG) as n:
                steps(D8 + n, 8, {4: lambda: z_piece_lo(n), 6: lambda: gate_side(0, n)})
                gate_side(1, n)
                gate_sum(n)
            z_piece_lo(NG)

            down(E8, 1, 1, False)
            hooks = boundary(PC_EF, NO_SPLIT, pre_gain(2), post_norm(1, 1.0))
            hooks[7] = pre_norm(2)
            gate_up(F8, PC_F, NO_SPLIT, U_F, 2, hooks)
            down(H8, 3, 2, True)
            update = post_norm(2, 0.5)
            for q in range(NG):
                update(q)


_INS = ["x", "ffn1_norm_pre", "ffn1_w_in", "ffn1_w_out", "ffn1_norm_post", "mix_norm_pre", "w_in",
        "diff_lambda", "diff_subln", "swa_sinks", "w_branch_diff", "w_branch_swa", "w_out",
        "mix_norm_post", "ffn2_norm_pre", "ffn2_w_in", "ffn2_w_out", "ffn2_norm_post"]


def kernel(**inputs):
    import concourse.bacc as bacc
    from concourse.bass_utils import run_bass_kernel_spmd

    nc = bacc.Bacc("TRN2", target_bir_lowering=False, num_devices=1)
    arrays, args = {}, []
    for name in _INS:
        a = np.ascontiguousarray(inputs[name])
        arrays[f"in_{name}"] = a
        args.append(nc.dram_tensor(f"in_{name}", a.shape, mybir.dt.from_np(a.dtype), kind="ExternalInput").ap())
    out = nc.dram_tensor("out_0", (1, SEQ, D_MODEL), F32, kind="ExternalOutput").ap()
    layer_kernel(nc, *args, out)
    r = run_bass_kernel_spmd(nc, [arrays], core_ids=[0])
    return r.results[0]["out_0"]
```

```python
from contextlib import ExitStack

import numpy as np

import concourse.bass as bass
from concourse import mybir

F32 = mybir.dt.float32
F32R = mybir.dt.float32r
BF16 = mybir.dt.bfloat16
ALU = mybir.AluOpType
ACT = mybir.ActivationFunctionType
AX = mybir.AxisListType

P = 128
CW = 512
D_MODEL, SEQ, D_FF = 2048, 256, 5504
MT = SEQ // P
KT = D_MODEL // P
FT = D_FF // P
HEADS, HD = 8, 64
SWA_HEADS, KV_HEADS = 16, 4
WIDTH = 1024
WINDOW = 128
EPS = 1e-6
LAM_INIT = 0.8 - 0.6 * 1.0
MASKED = 1e34

SUBS = 8
NG = D_MODEL // CW
PAIRS = D_FF // CW
TAIL = D_FF - PAIRS * CW
OUT_GROUPS = [4] * 7 + [3] * 5
assert sum(OUT_GROUPS) == FT
QKV_LOOPS, QKV_CHUNKS, GATE_CHUNKS = 3, 9, 8
UNITS = 16
LEAD = 3

A8 = 0
B8 = A8 + 2 * (PAIRS + 1)
C8 = B8 + NG * 3
G8 = C8 + QKV_CHUNKS
D8 = G8 + GATE_CHUNKS
E8 = D8 + NG
F8 = E8 + NG
H8 = F8 + 2 * (PAIRS + 1)
TOTAL_SUBS = 8 * (H8 + NG * 3)

PC_START = 0
PC_A = PC_START + 8
PC_BC = PC_A + 2 * (PAIRS + 1)
PC_QK = PC_BC + 8
PC_SK = PC_QK + 12
PC_O = PC_SK + 2
PC_D = PC_O + 8
PC_EF = PC_D + 2 * NG
PC_F = PC_EF + 8
NO_SPLIT = 14
SC_START, SC_BC, SC_O, SC_EF = 0, 8, 16, 20
U_B = PAIRS + 1
U_C = U_B + 2
U_G = [U_C + 5, U_C + 4]
U_D = [U_C + 9, U_C + 8]
U_E = [U_D[0] + NG, U_D[1] + NG]
U_F = [U_E[0] + 2, U_E[1] + 2]
U_H = [U_F[0] + PAIRS + 1, U_F[1] + PAIRS + 1]
R_PRE = [0, 2, 12]
R_POST = [1, 11, 13]
R_HEAD = 3
ROOTS = 14
Q_X, Q_Y, Q_O = [0, 16, 48], [8, 40, 56], 24
FULL_SUBS = [[2 * j, 2 * j + 1] for j in range(SUBS)]


ATT_CHUNKS = GATE_CHUNKS + 1
SK_UNIT = 2
O_TURN = 8 * ATT_CHUNKS - 2


def chunk_hooks(hooks, g):
    return {j: (lambda fs=hooks[8 * g + j]: [f() for f in fs]) for j in range(8) if 8 * g + j in hooks}


def out_subs():
    subs, k = [], 0
    for n in OUT_GROUPS:
        subs += [list(range(k, k + 2)), list(range(k + 2, k + n))]
        k += n
    return subs


HIDDEN_SUBS = out_subs()


def head_slope(n, i):
    return float(2.0 ** (-8.0 * (i + 1) / n))


def layer_kernel(nc, x, ffn1_norm_pre, ffn1_w_in, ffn1_w_out, ffn1_norm_post, mix_norm_pre, w_in,
                 diff_lambda, diff_subln, swa_sinks, w_branch_diff, w_branch_swa, w_out,
                 mix_norm_post, ffn2_norm_pre, ffn2_w_in, ffn2_w_out, ffn2_norm_post, out):
    with ExitStack() as ctx:
        base = (nc.sbuf_base + 31) // 32 * 32
        place = [base]

        def region(words):
            at = place[0]
            place[0] += 4 * words
            return at

        def sb(name, shape, dt, at):
            return nc.alloc_sbuf_tensor_at(name, shape, dt, offset=at)

        HALF = KT * P
        r_x = region(MT * D_MODEL)
        r_h = region(4 * HALF)
        r_act = region(2 * FT * SEQ)
        r_raw = region(4 * 4 * CW)
        r_hi = region(4 * 2 * CW)
        r_lo = region(4 * 2 * CW)
        r_stage = region(MT * CW)
        xs = sb("xs", [P, MT, D_MODEL], F32, r_x)
        h_hi = [sb(f"h_hi{m}", [P, KT, P], F32R, r_h + 8 * m * HALF) for m in range(MT)]
        h_lo = [sb(f"h_lo{m}", [P, KT, P], F32R, r_h + 8 * m * HALF + 4 * HALF) for m in range(MT)]
        y = [sb(f"y{m}", [P, D_MODEL], F32, r_h + 8 * m * HALF) for m in range(MT)]
        gain = sb("gain", [P, D_MODEL], F32, r_h + 12 * HALF)
        a_hi = sb("a_hi", [P, FT, SEQ], F32R, r_act)
        a_lo = sb("a_lo", [P, FT, SEQ], F32R, r_act + 4 * FT * SEQ)
        at = r_act
        qk = sb("qk", [P, 24, SEQ], F32, at)
        skt = sb("skt", [P, KV_HEADS, SEQ], F32, at + 4 * 24 * SEQ)
        dv = sb("dv", [P, MT, WIDTH], F32, at + 4 * 28 * SEQ)
        sv = sb("sv", [P, MT, KV_HEADS * HD], F32, at + 4 * 36 * SEQ)
        gates = sb("gates", [P, MT, 2 * D_MODEL], F32, at + 4 * 38 * SEQ)
        sc = sb("sc", [P, 2, 2, 3 * P], F32, at + 4 * 70 * SEQ)
        pt = sb("pt", [P, 2, 2, 3 * P], F32, at + 4 * 76 * SEQ)
        assert 82 * SEQ <= 2 * FT * SEQ
        z_hi = sb("z_hi", [P, KT, SEQ], F32R, at)
        z_lo = sb("z_lo", [P, KT, SEQ], F32R, at + 4 * KT * SEQ)
        raw = sb("raw", [P, 4, 4, CW], F32, r_raw)
        w_hi = sb("w_hi", [P, 4, 2, CW], F32R, r_hi)
        w_lo = sb("w_lo", [P, 4, 2, CW], F32R, r_lo)
        stage = sb("stage", [P, MT, CW], F32, r_stage)
        ident = sb("ident", [P, P], F32, region(P))
        dist = sb("dist", [P, 2, 3 * P], F32, region(6 * P))
        junk = sb("junk", [P, CW], BF16, region(CW // 2))
        rows = sb("rows", [P, P], F32, r_act)
        cols = sb("cols", [P, 3 * KT + 1], F32, region(56))
        lamp = sb("lamp", [P, 4, HD], F32, r_act + 4 * P)
        lprod = sb("lprod", [P, 2, HD], F32, r_act + 4 * P + 16 * HD)
        lsum = sb("lsum", [P, 2], F32, region(8))
        lexp = sb("lexp", [P, 2], F32, region(8))
        nlam = sb("nlam", [P, 1], F32, region(8))
        headgain = sb("headgain", [P, 1], F32, region(8))
        sink = sb("sink", [P, SWA_HEADS], F32, region(16))
        nsink = sb("nsink", [P, SWA_HEADS], F32, region(16))
        half = sb("half", [P, 2], F32, region(8))
        ssum = sb("ssum", [P, 2], F32, region(8))
        ssq = sb("ssq", [P, MT, NG], F32, region(8))
        ssx = sb("ssx", [P, MT, NG], F32, region(8))
        sso = sb("sso", [P, HEADS, MT], F32, region(16))
        var = sb("var", [P, ROOTS, MT], F32, region(32))
        root = sb("root", [P, ROOTS, MT], F32, region(32))
        qk_factor = sb("qk_factor", [P, QKV_LOOPS], F32, region(8))
        ssp = sb("ssp", [P, MT, 2], F32, region(8))
        nmax = sb("nmax", [P, 2, MT, 2], F32, region(8))
        tsink = sb("tsink", [P, 2, MT, 2], F32, region(8))
        esink = sb("esink", [P, 2, MT, 2], F32, region(8))
        sums = sb("sums", [P, 2, MT, 2], F32, region(8))
        rsum = sb("rsum", [P, 2, MT, 2], F32, region(8))
        mixw = sb("mixw", [P, 2, MT], F32, region(8))
        assert place[0] <= nc.sbuf_usable_end
        ctx.enter_context(nc.sbuf_tensor("arena", [P, (place[0] - base) // 4], F32))

        acc = ctx.enter_context(nc.psum_tensor("acc", [P, 2, MT, CW], F32))
        tp = ctx.enter_context(nc.psum_tensor("tp", [P, 4, CW], F32))

        def sem(name):
            return ctx.enter_context(nc.semaphore(name))

        x_in = [sem(f"x_in{q}") for q in range(NG)]
        rows_in = sem("rows_in")
        small_in = sem("small_in")
        gain_in = sem("gain_in")
        raw_in = [sem(f"raw_in{s}") for s in range(4)]
        out_written = sem("out_written")
        consts_made = sem("consts_made")
        gp_step = sem("gp_step")
        hi_ready = sem("hi_ready")
        lo_ready = sem("lo_ready")
        multiplied = sem("multiplied")
        acc_free = [sem("acc_free0"), sem("acc_free1")]
        turned = sem("turned")
        scaled = sem("scaled")
        piece_hi = sem("piece_hi")
        piece_out = sem("piece_out")
        squared = sem("squared")
        x_new = sem("x_new")
        var_ready = sem("var_ready")
        root_ready = sem("root_ready")
        cols_turned = sem("cols_turned")
        cols_copied = sem("cols_copied")
        lam_sums = sem("lam_sums")
        lam_exps = sem("lam_exps")
        sig_ready = sem("sig_ready")
        z_ready = sem("z_ready")
        scored = sem("scored")
        score_read = sem("score_read")
        nmax_ready = sem("nmax_ready")
        exp_ready = sem("exp_ready")
        mixed = sem("mixed")
        p_turned = sem("p_turned")
        p_copied = sem("p_copied")
        pv_done = sem("pv_done")
        o_read = sem("o_read")
        o_scaled = sem("o_scaled")
        dve_step = sem("dve_step")

        def bank(q, m):
            return (2 * q + m + 2) % 4

        w1_in, w1_out = ffn1_w_in[0], ffn1_w_out[0]
        w2_in, w2_out = ffn2_w_in[0], ffn2_w_out[0]
        x_d = x[0].rearrange("(m p) n -> p m n", p=P)
        out_d = out[0].rearrange("(m p) n -> p m n", p=P)
        block = ctx.enter_context(nc.Block())

        @block.sync
        def _(sp):
            def load(b8, j, w, row, tiles, col, width):
                if not (isinstance(b8, int) and 4 * b8 + j < 4):
                    sp.wait_ge(lo_ready, b8 * 8 + (2 * j - 6))
                src = w[row:row + tiles * P, bass.ds(col, width)].rearrange("(k p) n -> p k n", p=P)
                sp.dma_start(raw[:, j % 4, 0:tiles, 0:width], src).then_inc(raw_in[j % 4], 16)

            def chunk(b8, w, col, width=CW):
                for j in range(4):
                    load(b8, j, w, j * 4 * P, 4, col, width)

            def gate_up(b8, w, begun=False):
                def pair(i, width):
                    if not begun or not isinstance(i, int) or i > 0:
                        chunk(b8 + 2 * i, w, i * CW, width)
                    chunk(b8 + 2 * i + 1, w, D_FF + i * CW, width)
                pair(0, CW)
                with sp.Fori(1, PAIRS) as i:
                    pair(i, CW)
                pair(PAIRS, TAIL)

            def hidden_out(b8, w):
                with sp.Fori(0, NG) as n:
                    row = 0
                    for j, tiles in enumerate(OUT_GROUPS):
                        load(b8 + 3 * n, j, w, row * P, tiles, n * CW, CW)
                        row += tiles

            for q in range(NG):
                sp.dma_start(xs[:, :, q * CW:(q + 1) * CW], x_d[:, :, q * CW:(q + 1) * CW]).then_inc(x_in[q], 16)
                load(A8, q, w1_in, q * 4 * P, 4, 0, CW)
            gate_up(A8, w1_in, True)
            hidden_out(B8, w1_out)
            dv_col, sq_col = 2 * WIDTH, 3 * WIDTH
            with sp.Fori(0, 2) as i:
                for h in range(2):
                    chunk(C8 + 2 * i + h, w_in[0], i * WIDTH + h * CW)
            for c, col in enumerate([sq_col, sq_col + CW, dv_col, dv_col + CW]):
                chunk(C8 + 4 + c, w_in[0], col)
            with sp.Fori(0, 1 + GATE_CHUNKS) as c:
                chunk(C8 + 8 + c, w_in[0], c * CW + 4 * WIDTH)
            with sp.Fori(0, NG) as n:
                for j in range(4):
                    w = (w_branch_diff, w_branch_swa)[j // 2][0]
                    load(D8 + n, j, w, j % 2 * 4 * P, 4, n * CW, CW)
            with sp.Fori(0, NG) as n:
                chunk(E8 + n, w_out[0], n * CW)
            gate_up(F8, w2_in)
            hidden_out(H8, w2_out)
            for q in range(NG):
                sp.wait_ge(x_new, 4 * 2 * 2 + 2 * (q + 1))
                sp.dma_start(out_d[:, :, q * CW:(q + 1) * CW], xs[:, :, q * CW:(q + 1) * CW]).then_inc(out_written, 16)
            sp.wait_ge(out_written, 16 * NG)

        @block.gpsimd
        def _(gp):
            steps = [0]

            def link(ins):
                steps[0] += 1
                ins.then_inc(gp_step, 1)
                gp.wait_ge(gp_step, steps[0])

            link(nc.gpsimd.memset(ident[:], 0.0))
            nc.gpsimd.affine_select(out=ident[:], in_=ident[:], compare_op=ALU.not_equal, fill=1.0, base=0,
                                    pattern=[[-1, P]], channel_multiplier=1).then_inc(consts_made, 1)
            nc.gpsimd.memset(half[:], -0.5).then_inc(consts_made, 1)
            for kind in range(2):
                nc.gpsimd.iota(dist[:, kind, 0:P], pattern=[[-1, P]], base=0, channel_multiplier=1,
                               allow_small_or_imprecise_dtypes=True)
                link(nc.gpsimd.iota(dist[:, kind, P:3 * P], pattern=[[-1, 2 * P]], base=P, channel_multiplier=1,
                                    allow_small_or_imprecise_dtypes=True))
                for lo, n, b in ((0, P, 0), (P, 2 * P, P)):
                    d = dist[:, kind, lo:lo + n]
                    link(nc.gpsimd.affine_select(out=d, in_=d, compare_op=ALU.is_ge, fill=MASKED, base=b,
                                                 pattern=[[-1, n]], channel_multiplier=1))
                    if kind:
                        link(nc.gpsimd.affine_select(out=d, in_=d, compare_op=ALU.is_ge, fill=MASKED,
                                                     base=WINDOW - 1 - b, pattern=[[1, n]],
                                                     channel_multiplier=-1))
            for n in range(ROOTS):
                gp.wait_ge(var_ready, n + 1)
                if n == 0:
                    gp.wait_ge(consts_made, 2)
                nc.gpsimd.tensor_tensor(root[:, n, :], var[:, n, :], half[:], ALU.pow).then_inc(root_ready, 1)

        @block.tensor
        def _(pe):
            def chunk(b8, par, lhs, subs, width=CW, before=None, at=0):
                for j, tiles in enumerate(subs):
                    if before and j in before:
                        before[j]()
                    s = at + j
                    pe.wait_ge(lo_ready, b8 * 8 + (s + 1))
                    for t, k in enumerate(tiles):
                        first = j == 0 and t == 0
                        last = j == len(subs) - 1 and t == len(tiles) - 1
                        wh, wl = w_hi[:, s % 4, t, 0:width], w_lo[:, s % 4, t, 0:width]
                        for m in range(MT):
                            xh, xl = lhs(k, m)
                            o = acc[:, par, m, 0:width]
                            nc.tensor.matmul(o, xh, wh, start=first, stop=False)
                            nc.tensor.matmul(o, xh, wl, start=False, stop=False)
                            mm = nc.tensor.matmul(o, xl, wh, start=False, stop=last)
                    mm.then_inc(multiplied, 1)

            def from_h(k, m):
                return h_hi[m][:, k, :], h_lo[m][:, k, :]

            def from_a(k, m):
                return a_hi[:, k, m * P:(m + 1) * P], a_lo[:, k, m * P:(m + 1) * P]

            def from_z(k, m):
                return z_hi[:, k, m * P:(m + 1) * P], z_lo[:, k, m * P:(m + 1) * P]

            def turn(src, b, tiles):
                for t in range(tiles):
                    mm = nc.tensor.transpose(tp[:, b, t * P:(t + 1) * P], src(t), ident[:])
                mm.then_inc(turned, 1)

            def turn_stage(pieces, tiles=4):
                pe.wait_ge(piece_out, pieces)
                for m in range(MT):
                    turn(lambda t: stage[:, m, t * P:(t + 1) * P], m, tiles)

            def boundary(pc, ready, src):
                def quarter(q):
                    for m in range(MT):
                        ready(q, m)
                        if pc + 2 * q + m - 4 >= 0 and q >= 2:
                            pe.wait_ge(piece_out, pc + 2 * q + m - 3)
                        elif q < 2 and pc:
                            pe.wait_ge(piece_out, pc)
                        turn(lambda t: src(4 * q + t, m), bank(q, m), 4)

                def have(q):
                    pe.wait_ge(piece_out, pc + 2 * (q + 1))
                return {0: lambda: (quarter(0), quarter(1), have(0)), 2: lambda: (quarter(2), have(1)),
                        4: lambda: (quarter(3), have(2)), 6: lambda: have(3)}

            def x_tile(k, m):
                return xs[:, m, k * P:(k + 1) * P]

            def gate_up(b8, pc, uses, hooks):
                def pair(i, width, gate_hooks):
                    if not isinstance(i, int) or uses[0] + i > 0:
                        pe.wait_ge(acc_free[0], 2 * (uses[0] + i))
                    chunk(b8 + 2 * i, 0, from_h, FULL_SUBS, width, gate_hooks)
                    if not isinstance(i, int) or uses[1] + i > 0:
                        pe.wait_ge(acc_free[1], 2 * (uses[1] + i))
                    chunk(b8 + 2 * i + 1, 1, from_h, FULL_SUBS, width)

                def turn_last(i):
                    def hook():
                        pe.wait_ge(acc_free[1], 2 * (uses[1] + i))
                        turn_stage(pc + 2 * (i - 1))
                    return hook
                pair(0, CW, hooks)
                with pe.Fori(1, PAIRS) as i:
                    pair(i, CW, {1: turn_last(i)})
                pair(PAIRS, TAIL, {1: turn_last(PAIRS)})
                pe.wait_ge(acc_free[1], 2 * (uses[1] + PAIRS + 1))
                turn_stage(pc + 2 * PAIRS, TAIL // P)

            def down(b8, uses, lhs, subs, pieces, turn_last=None):
                def two(t, hook):
                    for par in range(2):
                        pe.wait_ge(acc_free[par], 2 * (uses[par] + t))
                        late = {len(subs) - 3 if len(subs) > 8 else 6: lambda: pe.wait_ge(piece_out, pieces)}
                        if hook and par == 0:
                            late[2] = hook
                        chunk(b8 + (2 * t + par) * (len(subs) // 8), par, lhs, subs, before=late)
                if turn_last:
                    two(0, turn_last)
                    two(1, None)
                else:
                    with pe.Fori(0, NG // 2) as t:
                        two(t, None)

            pe.wait_ge(rows_in, 16 * 4)
            pe.wait_ge(consts_made, 1)
            nc.tensor.transpose(tp[:, 0, 0:3 * KT + 1], rows[0:3 * KT + 1, :],
                                ident[0:3 * KT + 1, 0:3 * KT + 1]).then_inc(cols_turned, 1)
            pe.wait_ge(cols_copied, 1)

            gate_up(A8, PC_A, [0, 0],
                    boundary(PC_START, lambda q, m: pe.wait_ge(x_in[q], 16), x_tile))
            down(B8, [U_B, U_B], from_a, HIDDEN_SUBS, PC_BC)

            def turn_qk(c, par, i):
                def hook():
                    pe.wait_ge(acc_free[par], 2 * (U_C + i + 1))
                    turn_stage(PC_QK + 2 * c)
                return hook

            def qk_pair(i, first_hooks):
                for par in range(2):
                    pe.wait_ge(acc_free[par], 2 * (U_C + i))
                    chunk(C8 + 2 * i + par, par, from_h, FULL_SUBS,
                          before={2: turn_qk(2 * i, 0, i)} if par else first_hooks)

            qk_pair(0, boundary(PC_BC, lambda q, m: pe.wait_ge(x_new, 2 * q + m + 1), x_tile))
            with pe.Fori(1, QKV_LOOPS) as i:
                qk_pair(i, {2: turn_qk(2 * i - 1, 1, i - 1)})
            for c in range(6, QKV_CHUNKS - 1):
                pe.wait_ge(acc_free[c % 2], 2 * (U_C + c // 2))
                chunk(C8 + c, c % 2, from_h, FULL_SUBS, before={2: turn_qk(5, 1, 2)} if c == 6 else None)

            def scores(u):
                qt = u if u < HEADS else 16 + u - HEADS
                if u:
                    pe.wait_ge(score_read, u)
                if u in (0, SK_UNIT + 1):
                    pe.wait_ge(piece_out, PC_SK if u == 0 else PC_O)
                for m in range(MT):
                    for c in range(2):
                        r = slice(c * HD, (c + 1) * HD)
                        kt = qk[r, HEADS + u, :] if u < HEADS else skt[r, (u - HEADS) // 2, :]
                        mm = nc.tensor.matmul(tp[:, 2 + c, m * P:P + 2 * m * P], qk[r, qt, m * P:(m + 1) * P],
                                              kt[:, 0:(m + 1) * P], start=True, stop=True)
                mm.then_inc(scored, 1)

            def turn_p(u):
                pe.wait_ge(mixed, u + 1)
                if u:
                    pe.wait_ge(o_read, u)
                for c in range(1 if u < HEADS else 2):
                    for b in range(3):
                        mm = nc.tensor.transpose(tp[:, c, b * P:(b + 1) * P], sc[:, u % 2, c, b * P:(b + 1) * P],
                                                 ident[:])
                mm.then_inc(p_turned, 1)

            def pv(u):
                pe.wait_ge(p_copied, u + 1)
                if u == 0:
                    pe.wait_ge(acc_free[1], 2 * (U_C + 4))
                for c in range(1 if u < HEADS else 2):
                    n = P if u < HEADS else HD
                    for m in range(MT):
                        o = tp[:, m, 3 * P + c * HD:3 * P + c * HD + n]
                        for k in range(m + 1):
                            v = dv[:, k, u * P:(u + 1) * P] if u < HEADS else \
                                sv[:, k, (u - HEADS) // 2 * HD:(u - HEADS) // 2 * HD + HD]
                            b = m + k
                            mm = nc.tensor.matmul(o, pt[:, u % 2, c, b * P:(b + 1) * P], v,
                                                  start=(k == 0), stop=(k == m))
                mm.then_inc(pv_done, 1)

            hooks = {}
            for u in range(UNITS):
                hooks.setdefault(4 * u, []).append(lambda u=u: scores(u))
            for u in range(UNITS):
                hooks.setdefault(4 * u + 4, []).append(lambda u=u: turn_p(u))
                hooks.setdefault(4 * u + 6, []).append(lambda u=u: pv(u))

            def turn_sk():
                pe.wait_ge(acc_free[0], 2 * (U_C + QKV_CHUNKS // 2 + 1))
                pe.wait_ge(score_read, SK_UNIT + 1)
                for m in range(MT):
                    turn(lambda t: stage[:, m, t * P:(t + 1) * P], 2 + m, 4)
            hooks[4 * SK_UNIT + 2].insert(0, turn_sk)

            def o_tile(k, m):
                return qk[:, k if k < HEADS else 16 + k - HEADS, m * P:(m + 1) * P]

            def turn_o(q):
                def hook():
                    if q == 0:
                        pe.wait_ge(o_scaled, HEADS)
                        pe.wait_ge(o_read, UNITS)
                    for m in range(MT):
                        if q >= 2:
                            pe.wait_ge(piece_out, PC_O + 2 * q + m - 3)
                        turn(lambda t: o_tile(4 * q + t, m), bank(q, m), 4)
                return hook
            hooks.setdefault(O_TURN, []).append(turn_o(0))
            hooks.setdefault(O_TURN + 1, []).append(turn_o(1))
            for g in range(ATT_CHUNKS):
                c = QKV_CHUNKS - 1 + g
                pe.wait_ge(acc_free[c % 2], 2 * (U_C + c // 2))
                chunk(C8 + c, c % 2, from_h, FULL_SUBS, before=chunk_hooks(hooks, g))

            def branch(n, first, second):
                for par, hk in ((0, first), (1, second)):
                    pe.wait_ge(acc_free[par], 2 * (U_D[par] + n))
                    chunk(D8 + n, par, from_h, FULL_SUBS[4 * par:4 * par + 4], before=hk, at=4 * par)

            def turn_z(n):
                def hook():
                    pe.wait_ge(z_ready, 2 * n)
                    turn_stage(PC_D + 2 * (n - 1))
                return hook

            def have(q):
                pe.wait_ge(piece_out, PC_O + 2 * (q + 1))
            branch(0, {0: lambda: (have(0), turn_o(2)()), 2: lambda: (have(1), turn_o(3)())},
                   {0: lambda: have(2), 2: lambda: have(3)})
            with pe.Fori(1, NG) as n:
                branch(n, {2: turn_z(n)}, None)

            down(E8, U_E, from_z, FULL_SUBS, PC_EF, turn_z(NG))
            gate_up(F8, PC_F, U_F,
                    boundary(PC_EF, lambda q, m: pe.wait_ge(x_new, 8 + 2 * q + m + 1), x_tile))
            down(H8, U_H, from_a, HIDDEN_SUBS, PC_F + 2 * (PAIRS + 1))

        @block.scalar
        def _(act):
            def split(b8, j):
                s = j + LEAD
                if isinstance(b8, int) and 8 * b8 + s >= TOTAL_SUBS:
                    return
                g = s // 2
                if s % 2 == 0 or (isinstance(b8, int) and 8 * b8 + s < 4 and s % 2 == 0):
                    act.wait_ge(raw_in[g % 4], b8 * 16 + 16 * (g // 4 + 1))
                if not (isinstance(b8, int) and 8 * b8 + s < 4):
                    act.wait_ge(multiplied, b8 * 8 + (s - 3))
                nc.scalar.activation(w_hi[:, s % 4], raw[:, g % 4, s % 2 * 2:s % 2 * 2 + 2], ACT.Copy)\
                    .then_inc(hi_ready, 1)

            def steps(b8, n, before=None):
                for j in range(n):
                    if before and j in before:
                        before[j]()
                    split(b8, j)

            def await_turned(pc):
                return lambda: act.wait_ge(turned, pc + 2)

            def plain_hi(dst, tiles=4):
                for m in range(MT):
                    nc.scalar.activation(dst(m), tp[:, m, 0:tiles * P], ACT.Copy).then_inc(piece_hi, 1)

            def boundary(sc0):
                def quarter(q):
                    for m in range(MT):
                        act.wait_ge(scaled, sc0 + 2 * q + m + 1)
                        nc.scalar.activation(h_hi[m][:, 4 * q:4 * q + 4, :], stage[:, m, :], ACT.Copy).then_inc(piece_hi, 1)
                return {0: lambda: quarter(0), 1: lambda: quarter(1), 3: lambda: quarter(2), 5: lambda: quarter(3)}

            def square(n, src, total):
                if not (isinstance(n, int) and n == 0):
                    act.wait_ge(squared, n)
                nc.scalar.activation(junk[:, 0:src.shape[-1]], src, ACT.Square, accum_out=total)\
                    .then_inc(squared, 1)

            def square_x(k):
                def hook():
                    for m in range(MT):
                        for q in range(NG):
                            if k == 0:
                                act.wait_ge(x_in[q], 16)
                            square(Q_X[k] + m * NG + q, xs[:, m, q * CW:(q + 1) * CW], ssx[:, m, q:q + 1])
                return hook

            def gate_up(b8, pc, uses, k, hooks):
                def pair(i, width, gate_hooks):
                    steps(b8 + 2 * i, 8, gate_hooks)
                    if isinstance(i, int) and i == 0:
                        act.wait_ge(root_ready, R_PRE[k] + 1)
                    act.wait_ge(turned, pc + 2 * i)
                    act.wait_ge(multiplied, (b8 + 2 * i) * 8 + 8)
                    for m in range(MT):
                        nc.scalar.activation(stage[:, m, 0:width], acc[:, 0, m, 0:width], ACT.Silu,
                                             scale=root[:, R_PRE[k], m:m + 1]).then_inc(acc_free[0], 1)
                    steps(b8 + 2 * i + 1, 8)

                def last_hi(i):
                    return {4: await_turned(pc + 2 * (i - 1)),
                            5: lambda: plain_hi(lambda m: a_hi[:, bass.ds(4 * (i - 1), 4), m * P:(m + 1) * P])}
                pair(0, CW, hooks)
                with act.Fori(1, PAIRS) as i:
                    pair(i, CW, last_hi(i))
                pair(PAIRS, TAIL, last_hi(PAIRS))
                n = TAIL // P
                await_turned(pc + 2 * PAIRS)()
                plain_hi(lambda m: a_hi[:, 4 * PAIRS:4 * PAIRS + n, m * P:(m + 1) * P], n)

            def down(b8, units, k, g_d, first=None, last=False):
                act.wait_ge(multiplied, 8 * b8)
                act.dma_start(gain[:], g_d[0:1, :].partition_broadcast(P)).then_inc(gain_in, 16)

                def two(t):
                    for par in range(2):
                        n8 = b8 + (2 * t + par) * units
                        steps(n8, 8 * units, first if isinstance(t, int) and t + par == 0 else None)
                        act.wait_ge(multiplied, (n8 + units) * 8)
                        for m in range(MT):
                            square((2 * t + par) * 2 + (Q_Y[k] + m), acc[:, par, m, :], ssp[:, m, par:par + 1])
                if last or first:
                    two(0)
                    two(1)
                else:
                    with act.Fori(0, NG // 2) as t:
                        two(t)

            for k, g in enumerate((ffn1_norm_pre, mix_norm_pre, ffn2_norm_pre)):
                act.dma_start(rows[k * KT:(k + 1) * KT, :], g[0].rearrange("(t p) -> t p", p=P)).then_inc(rows_in, 16)
            act.dma_start(rows[3 * KT:3 * KT + 1, :], diff_subln[0:1, :]).then_inc(rows_in, 16)
            act.dma_start(lamp[:], diff_lambda.rearrange("a b c -> a (b c)").partition_broadcast(P)).then_inc(small_in, 16)
            act.dma_start(sink[:], swa_sinks[0:1, :].partition_broadcast(P)).then_inc(small_in, 16)
            for j in range(-LEAD, 0):
                split(0, j)

            hooks = boundary(SC_START)
            hooks[6] = square_x(0)
            gate_up(A8, PC_A, [0, 0], 0, hooks)
            down(B8, 3, 0, ffn1_norm_post)

            def to_stage(par, c):
                act.wait_ge(turned, PC_QK + 2 * c)
                act.wait_ge(multiplied, (C8 + c) * 8 + 8)
                for m in range(MT):
                    nc.scalar.activation(stage[:, m, :], acc[:, par, m, :], ACT.Copy,
                                         scale=root[:, R_PRE[1], m:m + 1]).then_inc(acc_free[par], 1)

            def qk_pair(i, hooks):
                for par in range(2):
                    steps(C8 + 2 * i + par, 8, None if par else hooks)
                    if isinstance(i, int) and i == 0 and par == 0:
                        act.wait_ge(root_ready, R_PRE[1] + 1)
                    to_stage(par, 2 * i + par)
            hooks = boundary(SC_BC)
            hooks[6] = square_x(1)
            qk_pair(0, hooks)
            with act.Fori(1, QKV_LOOPS) as i:
                qk_pair(i, None)
            act.wait_ge(lam_sums, 1)
            nc.scalar.activation(lexp[:], lsum[:], ACT.Exp).then_inc(lam_exps, 1)
            rs = R_PRE[1]
            for c in (6, 7):
                steps(C8 + c, 8)
                act.wait_ge(multiplied, (C8 + c) * 8 + 8)
                for m in range(MT):
                    nc.scalar.activation(dv[:, m, (c - 6) * CW:(c - 5) * CW], acc[:, c % 2, m, :], ACT.Copy,
                                         scale=root[:, rs, m:m + 1]).then_inc(acc_free[c % 2], 1)
            def exps(u):
                act.wait_ge(nmax_ready, u + 1)
                b = u % 2
                for c in range(2):
                    for m in range(MT):
                        s = sc[:, b, c, m * P:P + 2 * m * P]
                        ins = nc.scalar.activation(s, s, ACT.Exp, bias=nmax[:, b, m, c:c + 1],
                                                   accum_out=sums[:, b, m, c:c + 1])
                if u >= HEADS:
                    ins = nc.scalar.activation(esink[:, b], tsink[:, b], ACT.Exp)
                ins.then_inc(exp_ready, 1)

            def copy_p(u):
                act.wait_ge(p_turned, u + 1)
                if u >= 2:
                    act.wait_ge(pv_done, u - 1)
                n = 1 if u < HEADS else 2
                nc.scalar.activation(pt[:, u % 2, 0:n], tp[:, 0:n, 0:3 * P], ACT.Copy).then_inc(p_copied, 1)

            def square_o(u):
                act.wait_ge(o_read, u + 1)
                for m in range(MT):
                    square(Q_O + 2 * u + m, qk[:, u, m * P:(m + 1) * P], sso[:, u, m:m + 1])

            hooks = {}
            for u in range(UNITS):
                hooks.setdefault(4 * u + 1, []).append(lambda u=u: exps(u))
                hooks.setdefault(4 * u + 5, []).append(lambda u=u: copy_p(u))
                if u < HEADS:
                    hooks.setdefault(4 * u + 9, []).append(lambda u=u: square_o(u))

            def o_hi(q):
                def hook():
                    act.wait_ge(multiplied, 8 * D8 - 4 if q < 2 else 8 * D8)
                    for m in range(MT):
                        if q >= 2:
                            act.wait_ge(turned, PC_O + 2 * q + m + 1)
                            src = tp[:, bank(q, m), :]
                        else:
                            act.wait_ge(scaled, SC_O + 2 * q + m + 1)
                            src = stage[:, m, :]
                        nc.scalar.activation(h_hi[m][:, 4 * q:4 * q + 4, :], src, ACT.Copy).then_inc(piece_hi, 1)
                return hook
            hooks.setdefault(O_TURN + 1, []).append(o_hi(0))
            KW = KV_HEADS * HD
            for g in range(ATT_CHUNKS):
                c = QKV_CHUNKS - 1 + g
                steps(C8 + c, 8, chunk_hooks(hooks, g))
                act.wait_ge(multiplied, (C8 + c) * 8 + 8)
                for m in range(MT):
                    if g:
                        nc.scalar.activation(gates[:, m, (g - 1) * CW:g * CW], acc[:, c % 2, m, :], ACT.Copy,
                                             scale=root[:, rs, m:m + 1]).then_inc(acc_free[c % 2], 1)
                        continue
                    dup = stage[:, m, :].rearrange("p (h two d) -> p h two d", two=2, d=HD)
                    for two in range(2):
                        nc.scalar.activation(dup[:, :, two, :], acc[:, 0, m, 0:KW].rearrange("p (h d) -> p h d", d=HD),
                                             ACT.Copy, scale=root[:, rs, m:m + 1])
                    nc.scalar.activation(sv[:, m, :], acc[:, 0, m, KW:2 * KW], ACT.Copy,
                                         scale=root[:, rs, m:m + 1]).then_inc(acc_free[0], 1)

            def sigmoids(n):
                def hook():
                    for m in range(MT):
                        for side in range(2):
                            g = gates[:, m, bass.ds(side * D_MODEL + n * CW, CW)]
                            nc.scalar.activation(g, g, ACT.Sigmoid).then_inc(sig_ready, 1)
                return hook

            def z_piece_hi(n):
                plain_hi(lambda m: z_hi[:, bass.ds(4 * (n - 1), 4), m * P:(m + 1) * P])
            act.wait_ge(acc_free[0], 2 * U_D[0])
            act.wait_ge(acc_free[1], 2 * U_D[1])
            steps(D8, 8, {0: o_hi(1), 1: o_hi(2), 3: o_hi(3), 4: sigmoids(0)})
            with act.Fori(1, NG) as n:
                steps(D8 + n, 8, {2: sigmoids(n), 5: await_turned(PC_D + 2 * (n - 1)),
                                  6: lambda: z_piece_hi(n)})

            down(E8, 1, 1, mix_norm_post, {5: await_turned(PC_D + 2 * (NG - 1)), 6: lambda: z_piece_hi(NG)})
            hooks = boundary(SC_EF)
            hooks[6] = square_x(2)
            gate_up(F8, PC_F, U_F, 2, hooks)
            down(H8, 3, 2, ffn2_norm_post, last=True)

        @block.vector
        def _(dve):
            chain = [0]

            def link(ins):
                chain[0] += 1
                ins.then_inc(dve_step, 1)
                dve.wait_ge(dve_step, chain[0])

            def split(b8, j):
                s = j + LEAD
                if isinstance(b8, int) and 8 * b8 + s >= TOTAL_SUBS:
                    return
                g = s // 2
                dve.wait_ge(hi_ready, b8 * 8 + (s + 1))
                nc.vector.tensor_tensor(w_lo[:, s % 4], raw[:, g % 4, s % 2 * 2:s % 2 * 2 + 2],
                                        w_hi[:, s % 4].bitcast(F32), ALU.subtract).then_inc(lo_ready, 1)

            def steps(b8, n, before=None):
                for j in range(n):
                    if before and j in before:
                        before[j]()
                    split(b8, j)

            def plain_lo(pc, skip, hi, lo, tiles=4):
                for m in range(MT):
                    dve.wait_ge(piece_hi, pc - skip + m + 1)
                    nc.vector.tensor_tensor(lo(m), tp[:, m, 0:tiles * P].rearrange("p (t n) -> p t n", n=P),
                                            hi(m).bitcast(F32), ALU.subtract).then_inc(piece_out, 1)

            def quarters(pc, skip, gains):
                def quarter(q):
                    for m in range(MT):
                        g = gains(q)
                        if g is None:
                            continue
                        dve.wait_ge(turned, pc + 2 * q + m + 1)
                        if q:
                            dve.wait_ge(piece_out, pc + 2 * q + m - 1)
                        nc.vector.tensor_tensor(stage[:, m, :].rearrange("p (t n) -> p t n", n=P),
                                                tp[:, bank(q, m), :].rearrange("p (t n) -> p t n", n=P), g,
                                                ALU.mult).then_inc(scaled, 1)
                    for m in range(MT):
                        dve.wait_ge(piece_hi, pc - skip + 2 * q + m + 1)
                        src = stage[:, m, :] if gains(q) is not None else tp[:, bank(q, m), :]
                        nc.vector.tensor_tensor(h_lo[m][:, 4 * q:4 * q + 4, :], src.rearrange("p (t n) -> p t n", n=P),
                                                h_hi[m][:, 4 * q:4 * q + 4, :].bitcast(F32),
                                                ALU.subtract).then_inc(piece_out, 1)

                return quarter

            def boundary(pc, skip, gains, update=None):
                quarter = quarters(pc, skip, gains)

                def new_x(q):
                    if update:
                        update(q)
                return {0: lambda: (new_x(0), new_x(1), quarter(0)), 1: lambda: (new_x(2), quarter(1)),
                        3: lambda: (new_x(3), quarter(2)), 5: lambda: quarter(3)}

            def pre_gain(k):
                return lambda q: cols[:, k * KT + 4 * q:k * KT + 4 * q + 4].unsqueeze(2).to_broadcast([P, 4, P])

            def variance(n, total, width, factor=1.0):
                nc.vector.tensor_scalar(var[:, n, :], total, 1.0 / (width * factor ** 2), EPS / factor ** 2,
                                        ALU.mult, ALU.add).then_inc(var_ready, 1)

            def pre_norm(k):
                def hook():
                    dve.wait_ge(squared, Q_X[k] + 8)
                    link(nc.vector.tensor_reduce(ssum[:], ssx[:], AX.X, ALU.add))
                    variance(R_PRE[k], ssum[:], D_MODEL)
                return hook

            def post_norm(k, factor):
                dve.wait_ge(acc_free[1], 2 * (U_C, U_F[1], U_H[1] + 2)[k])
                link(nc.vector.tensor_reduce(ssum[:], ssq[:], AX.X, ALU.add))
                variance(R_POST[k], ssum[:], D_MODEL, factor)

                def update(q):
                    if q == 0:
                        dve.wait_ge(root_ready, R_POST[k] + 1)
                    for m in range(MT):
                        c = slice(q * CW, (q + 1) * CW)
                        nc.vector.scalar_tensor_tensor(out=xs[:, m, c], in0=y[m][:, c],
                                                       scalar=root[:, R_POST[k], m:m + 1], in1=xs[:, m, c],
                                                       op0=ALU.mult, op1=ALU.add).then_inc(x_new, 1)
                return update

            def gate_up(b8, pc, skip, uses, k, hooks):
                def pair(i, width, gate_hooks):
                    steps(b8 + 2 * i, 8, gate_hooks)
                    steps(b8 + 2 * i + 1, 8)
                    dve.wait_ge(multiplied, (b8 + 2 * i) * 8 + 16)
                    dve.wait_ge(acc_free[0], 2 * (uses[0] + i + 1))
                    for m in range(MT):
                        nc.vector.scalar_tensor_tensor(out=stage[:, m, 0:width], in0=acc[:, 1, m, 0:width],
                                                       scalar=root[:, R_PRE[k], m:m + 1],
                                                       in1=stage[:, m, 0:width],
                                                       op0=ALU.mult, op1=ALU.mult).then_inc(acc_free[1], 1)

                def last_lo(i):
                    return lambda: plain_lo(pc + 2 * (i - 1), skip,
                                            lambda m: a_hi[:, bass.ds(4 * (i - 1), 4), m * P:(m + 1) * P],
                                            lambda m: a_lo[:, bass.ds(4 * (i - 1), 4), m * P:(m + 1) * P])
                pair(0, CW, hooks)
                with dve.Fori(1, PAIRS) as i:
                    pair(i, CW, {4: last_lo(i)})
                pair(PAIRS, TAIL, {4: last_lo(PAIRS)})
                n = TAIL // P
                plain_lo(pc + 2 * PAIRS, skip, lambda m: a_hi[:, 4 * PAIRS:4 * PAIRS + n, m * P:(m + 1) * P],
                         lambda m: a_lo[:, 4 * PAIRS:4 * PAIRS + n, m * P:(m + 1) * P], n)

            def down(b8, units, k, first=None, last=False):
                def two(t):
                    for par in range(2):
                        n8 = b8 + (2 * t + par) * units
                        steps(n8, 8 * units, first if isinstance(t, int) and t + par == 0 else None)
                        dve.wait_ge(gain_in, 16 * (k + 1))
                        for m in range(MT):
                            dve.wait_ge(squared, (2 * t + par) * 2 + (Q_Y[k] + m + 1))
                            nc.vector.tensor_copy(ssq[:, m, bass.ds(2 * t + par, 1)], ssp[:, m, par:par + 1])
                            nc.vector.tensor_tensor(y[m][:, bass.ds((2 * t + par) * CW, CW)], acc[:, par, m, :],
                                                    gain[:, bass.ds((2 * t + par) * CW, CW)],
                                                    ALU.mult).then_inc(acc_free[par], 1)
                if last or first:
                    two(0)
                    two(1)
                else:
                    with dve.Fori(0, NG // 2) as t:
                        two(t)

            dve.wait_ge(cols_turned, 1)
            nc.vector.tensor_copy(cols[:], tp[:, 0, 0:3 * KT + 1]).then_inc(cols_copied, 1)
            dve.wait_ge(cols_copied, 1)
            nc.vector.tensor_scalar(headgain[:], cols[:, 3 * KT:3 * KT + 1], 1.0 - LAM_INIT, None, ALU.mult)
            for j in range(-LEAD, 0):
                split(0, j)

            def lambda_sums():
                dve.wait_ge(small_in, 16 * 2)
                nc.vector.tensor_tensor(lprod[:, 0, :], lamp[:, 0, :], lamp[:, 1, :], ALU.mult)
                link(nc.vector.tensor_tensor(lprod[:, 1, :], lamp[:, 2, :], lamp[:, 3, :], ALU.mult))
                nc.vector.tensor_reduce(lsum[:], lprod[:], AX.X, ALU.add).then_inc(lam_sums, 1)
                link(nc.vector.tensor_scalar(nsink[:], sink[:], -1.0, None, ALU.mult))

            hooks = boundary(PC_START, 0, pre_gain(0))
            hooks[6] = lambda_sums
            hooks[7] = pre_norm(0)
            gate_up(A8, PC_A, 0, [0, 0], 0, hooks)
            down(B8, 3, 0)

            hooks = boundary(PC_BC, 0, pre_gain(1), post_norm(0, 0.5))
            hooks[7] = pre_norm(1)

            for i in range(QKV_LOOPS):
                ins = nc.vector.memset(qk_factor[:, i:i + 1], 1.0 if i == 1 else HD ** -0.5)
            link(ins)

            def take_qk(c, i):
                def hook():
                    for m in range(MT):
                        dve.wait_ge(turned, PC_QK + 2 * c + m + 1)
                        nc.vector.tensor_scalar(qk[:, bass.ds(4 * c, 4), m * P:(m + 1) * P],
                                                tp[:, m, :].rearrange("p (t n) -> p t n", n=P),
                                                qk_factor[:, bass.ds(i, 1)], None, ALU.mult).then_inc(piece_out, 1)
                return hook

            def qk_pair(i, first_hooks):
                steps(C8 + 2 * i, 8, first_hooks)
                steps(C8 + 2 * i + 1, 8, {4: take_qk(2 * i, i)})
            qk_pair(0, hooks)
            with dve.Fori(1, QKV_LOOPS) as i:
                qk_pair(i, {4: take_qk(2 * i - 1, i - 1)})
            steps(C8 + 6, 8, {4: take_qk(5, 2)})
            dve.wait_ge(lam_exps, 1)
            link(nc.vector.tensor_tensor(nlam[:], lexp[:, 1:2], lexp[:, 0:1], ALU.subtract))
            link(nc.vector.tensor_scalar(nlam[:], nlam[:], -LAM_INIT, None, ALU.add))
            steps(C8 + 7, 8)

            def scores_read(u):
                b = u % 2
                dve.wait_ge(scored, u + 1)
                if u >= 2:
                    dve.wait_ge(p_turned, u - 1)
                if u < HEADS:
                    ins = nc.vector.scalar_tensor_tensor(
                        out=sc[:, b], in0=dist[:, 0:1, :].to_broadcast([P, 2, 3 * P]), scalar=-head_slope(HEADS, u),
                        in1=tp[:, 2:4, 0:3 * P], op0=ALU.mult, op1=ALU.add)
                else:
                    for c in range(2):
                        ins = nc.vector.scalar_tensor_tensor(
                            out=sc[:, b, c], in0=dist[:, 1, :],
                            scalar=-head_slope(SWA_HEADS, 2 * (u - HEADS) + c),
                            in1=tp[:, 2 + c, 0:3 * P], op0=ALU.mult, op1=ALU.add)
                ins.then_inc(score_read, 1)
                dve.wait_ge(score_read, u + 1)
                for m in range(MT):
                    ins = nc.vector.tensor_reduce(nmax[:, b, m, :], sc[:, b, :, m * P:P + 2 * m * P], AX.X,
                                                  ALU.max, negate=True)
                if u >= HEADS:
                    link(ins)
                    h = 2 * (u - HEADS)
                    link(nc.vector.tensor_tensor(nmax[:, b], nmax[:, b],
                                                 nsink[:, h:h + 2].unsqueeze(1).to_broadcast([P, MT, 2]), ALU.min))
                    ins = nc.vector.tensor_tensor(tsink[:, b], nmax[:, b],
                                                  sink[:, h:h + 2].unsqueeze(1).to_broadcast([P, MT, 2]), ALU.add)
                ins.then_inc(nmax_ready, 1)

            def mix(u):
                b = u % 2
                dve.wait_ge(exp_ready, u + 1)
                if u < HEADS:
                    link(nc.vector.reciprocal(rsum[:, b], sums[:, b]))
                    link(nc.vector.scalar_tensor_tensor(out=mixw[:, b], in0=sums[:, b, :, 0], scalar=nlam[:],
                                                        in1=rsum[:, b, :, 1], op0=ALU.mult, op1=ALU.mult))
                    for m in range(MT):
                        r = slice(m * P, P + 2 * m * P)
                        ins = nc.vector.scalar_tensor_tensor(out=sc[:, b, 0, r], in0=sc[:, b, 1, r],
                                                             scalar=mixw[:, b, m:m + 1], in1=sc[:, b, 0, r],
                                                             op0=ALU.mult, op1=ALU.add)
                else:
                    link(nc.vector.tensor_tensor(sums[:, b], sums[:, b], esink[:, b], ALU.add))
                    ins = nc.vector.reciprocal(rsum[:, b], sums[:, b])
                ins.then_inc(mixed, 1)

            def take_o(u):
                b = u % 2
                dve.wait_ge(pv_done, u + 1)
                dve.wait_ge(mixed, u + 1)
                if u < HEADS:
                    ins = nc.vector.tensor_tensor(qk[:, u, :].rearrange("p (m n) -> p m n", n=P),
                                                  tp[:, 0:2, 3 * P:4 * P],
                                                  rsum[:, b, :, 0:1].to_broadcast([P, MT, P]), ALU.mult)
                else:
                    ins = nc.vector.tensor_tensor(
                        qk[:, 16 + u - HEADS, :].rearrange("p (m c n) -> p m c n", c=2, n=HD),
                        tp[:, 0:2, 3 * P:4 * P].rearrange("p m (c n) -> p m c n", n=HD),
                        rsum[:, b].unsqueeze(3).to_broadcast([P, MT, 2, HD]), ALU.mult)
                ins.then_inc(o_read, 1)

            def head_var(u):
                dve.wait_ge(squared, Q_O + 2 * u + 2)
                variance(R_HEAD + u, sso[:, u, :], 2 * HD)

            def head_scale(u):
                dve.wait_ge(root_ready, R_HEAD + u + 1)
                dve.wait_ge(o_read, u + 1)
                o = qk[:, u, :].rearrange("p (m n) -> p m n", n=P)
                nc.vector.tensor_tensor(o, o, root[:, R_HEAD + u, :].unsqueeze(2).to_broadcast([P, MT, P]),
                                        ALU.mult).then_inc(o_scaled, 1)

            def take_sk():
                for m in range(MT):
                    dve.wait_ge(turned, PC_SK + m + 1)
                    nc.vector.tensor_copy(skt[:, :, m * P:(m + 1) * P],
                                          tp[:, 2 + m, :].rearrange("p (t n) -> p t n", n=P)).then_inc(piece_out, 1)

            hooks = {}
            for u in range(UNITS):
                hooks.setdefault(4 * u + 1, []).append(lambda u=u: scores_read(u))
                hooks.setdefault(4 * u + 3, []).append(lambda u=u: mix(u))
                hooks.setdefault(4 * u + 7, []).append(lambda u=u: take_o(u))
                if u < HEADS:
                    hooks.setdefault(4 * u + 10, []).append(lambda u=u: head_var(u))
                    hooks.setdefault(4 * u + 12, []).append(lambda u=u: head_scale(u))
            hooks[4 * SK_UNIT + 3].insert(0, take_sk)

            def head_gain(q):
                return headgain[:, 0:1].unsqueeze(2).to_broadcast([P, 4, P]) if q < 2 else None
            o_quarters = quarters(PC_O, NO_SPLIT, head_gain)
            hooks.setdefault(O_TURN + 1, []).append(lambda: o_quarters(0))
            for g in range(ATT_CHUNKS):
                steps(G8 - 1 + g, 8, chunk_hooks(hooks, g))

            def gate_side(side, n):
                dve.wait_ge(multiplied, (D8 + n) * 8 + 4 * (side + 1))
                dve.wait_ge(sig_ready, 4 * n + 4)
                for m in range(MT):
                    g = gates[:, m, bass.ds(side * D_MODEL + n * CW, CW)]
                    nc.vector.tensor_tensor(g, g, acc[:, side, m, :], ALU.mult).then_inc(acc_free[side], 1)

            def gate_sum(n):
                if not (isinstance(n, int) and n == 0):
                    dve.wait_ge(turned, PC_D + 2 * n)
                dve.wait_ge(acc_free[1], 2 * (U_D[1] + 1 + n))
                for m in range(MT):
                    nc.vector.tensor_tensor(stage[:, m, :], gates[:, m, bass.ds(n * CW, CW)],
                                            gates[:, m, bass.ds(D_MODEL + n * CW, CW)],
                                            ALU.add).then_inc(z_ready, 1)

            def z_piece_lo(n):
                plain_lo(PC_D + 2 * (n - 1), NO_SPLIT,
                         lambda m: z_hi[:, bass.ds(4 * (n - 1), 4), m * P:(m + 1) * P],
                         lambda m: z_lo[:, bass.ds(4 * (n - 1), 4), m * P:(m + 1) * P])
            steps(D8, 8, {0: lambda: o_quarters(1), 1: lambda: o_quarters(2), 3: lambda: o_quarters(3),
                          6: lambda: gate_side(0, 0)})
            gate_side(1, 0)
            gate_sum(0)
            with dve.Fori(1, NG) as n:
                steps(D8 + n, 8, {6: lambda: z_piece_lo(n), 7: lambda: gate_side(0, n)})
                gate_side(1, n)
                gate_sum(n)

            down(E8, 1, 1, {6: lambda: z_piece_lo(NG)})
            hooks = boundary(PC_EF, NO_SPLIT, pre_gain(2), post_norm(1, 1.0))
            hooks[7] = pre_norm(2)
            gate_up(F8, PC_F, NO_SPLIT, U_F, 2, hooks)
            down(H8, 3, 2, last=True)
            update = post_norm(2, 0.5)
            for q in range(NG):
                update(q)


_INS = ["x", "ffn1_norm_pre", "ffn1_w_in", "ffn1_w_out", "ffn1_norm_post", "mix_norm_pre", "w_in",
        "diff_lambda", "diff_subln", "swa_sinks", "w_branch_diff", "w_branch_swa", "w_out",
        "mix_norm_post", "ffn2_norm_pre", "ffn2_w_in", "ffn2_w_out", "ffn2_norm_post"]


def kernel(**inputs):
    import concourse.bacc as bacc
    from concourse.bass_utils import run_bass_kernel_spmd

    nc = bacc.Bacc("TRN2", target_bir_lowering=False, num_devices=1)
    arrays, args = {}, []
    for name in _INS:
        a = np.ascontiguousarray(inputs[name])
        arrays[f"in_{name}"] = a
        args.append(nc.dram_tensor(f"in_{name}", a.shape, mybir.dt.from_np(a.dtype), kind="ExternalInput").ap())
    out = nc.dram_tensor("out_0", (1, SEQ, D_MODEL), F32, kind="ExternalOutput").ap()
    layer_kernel(nc, *args, out)
    r = run_bass_kernel_spmd(nc, [arrays], core_ids=[0])
    return r.results[0]["out_0"]
```

```python
from contextlib import ExitStack

import numpy as np

import concourse.bass as bass
from concourse import mybir

F32 = mybir.dt.float32
F32R = mybir.dt.float32r
BF16 = mybir.dt.bfloat16
ALU = mybir.AluOpType
ACT = mybir.ActivationFunctionType
AX = mybir.AxisListType

P = 128
CW = 512
D_MODEL, SEQ, D_FF = 2048, 256, 5504
MT = SEQ // P
KT = D_MODEL // P
FT = D_FF // P
HEADS, HD = 8, 64
SWA_HEADS, KV_HEADS = 16, 4
WIDTH = 1024
WINDOW = 128
EPS = 1e-6
LAM_INIT = 0.8 - 0.6 * 1.0
MASKED = 1e34

SUBS = 8
NG = D_MODEL // CW
PAIRS = D_FF // CW
TAIL = D_FF - PAIRS * CW
OUT_GROUPS = [3] * 5 + [4] * 7
assert sum(OUT_GROUPS) == FT
QKV_LOOPS, QKV_CHUNKS, GATE_CHUNKS = 3, 9, 8
UNITS = 16
LEAD = 3

A8 = 0
B8 = A8 + 2 * (PAIRS + 1)
C8 = B8 + NG * 3
G8 = C8 + QKV_CHUNKS
D8 = G8 + GATE_CHUNKS
E8 = D8 + NG
F8 = E8 + NG
H8 = F8 + 2 * (PAIRS + 1)
TOTAL_SUBS = 8 * (H8 + NG * 3)

PC_START = 0
PC_A = PC_START + 8
PC_BC = PC_A + 2 * (PAIRS + 1)
PC_QK = PC_BC + 8
PC_SK = PC_QK + 12
PC_O = PC_SK + 2
PC_D = PC_O + 8
PC_EF = PC_D + 2 * NG
PC_F = PC_EF + 8
NO_SPLIT = 14
PC_PRE, SKIP_PRE = [PC_START, PC_BC, PC_EF], [0, 0, NO_SPLIT]
SC_START, SC_BC, SC_O, SC_EF = 0, 8, 16, 20
U_B = PAIRS + 1
U_C = U_B + 2
U_G = [U_C + 5, U_C + 4]
U_D = [U_C + 9, U_C + 8]
U_E = [U_D[0] + NG, U_D[1] + NG]
U_F = [U_E[0] + 2, U_E[1] + 2]
U_H = [U_F[0] + PAIRS + 1, U_F[1] + PAIRS + 1]
R_PRE = [0, 2, 12]
R_POST = [1, 11, 13]
R_HEAD = 3
ROOTS = 14
ROOT_STEPS = [(n, m) for n in range(ROOTS) for m in ((0, 1) if n in R_POST else (None,))]


def root_count(n, m=None):
    return ROOT_STEPS.index((n, m)) + 1


SKEW = 4
PIECES = [(0, 0), (1, 0), (0, 1), (1, 1), (2, 0), (2, 1), (3, 0), (3, 1)]
DVE_PIECES = 2
Y_RUNS = [(1, 0, 1), (1, 1, 2), (0, 2, 4), (1, 2, 4)]
Q_X, Q_Y, Q_O = [0, 16, 48], [8, 40, 56], 24
FULL_SUBS = [[2 * j, 2 * j + 1] for j in range(SUBS)]


ATT_CHUNKS = GATE_CHUNKS + 1
SK_UNIT = 2
O_TURN = 8 * ATT_CHUNKS - 4


def chunk_hooks(hooks, g):
    return {j: (lambda fs=hooks[8 * g + j]: [f() for f in fs]) for j in range(8) if 8 * g + j in hooks}


def out_subs():
    subs, k = [], 0
    for n in OUT_GROUPS:
        subs += [list(range(k, k + 2)), list(range(k + 2, k + n))]
        k += n
    return subs


HIDDEN_SUBS = out_subs()


def head_slope(n, i):
    return float(2.0 ** (-8.0 * (i + 1) / n))


def layer_kernel(nc, x, ffn1_norm_pre, ffn1_w_in, ffn1_w_out, ffn1_norm_post, mix_norm_pre, w_in,
                 diff_lambda, diff_subln, swa_sinks, w_branch_diff, w_branch_swa, w_out,
                 mix_norm_post, ffn2_norm_pre, ffn2_w_in, ffn2_w_out, ffn2_norm_post, out):
    with ExitStack() as ctx:
        base = (nc.sbuf_base + 31) // 32 * 32
        place = [base]

        def region(words):
            at = place[0]
            place[0] += 4 * words
            return at

        def sb(name, shape, dt, at):
            return nc.alloc_sbuf_tensor_at(name, shape, dt, offset=at)

        HALF = KT * P
        r_x = region(MT * D_MODEL)
        r_h = region(4 * HALF)
        r_act = region(2 * FT * SEQ)
        r_raw = region(4 * 4 * CW)
        r_hi = region(4 * 2 * CW)
        r_lo = region(4 * 2 * CW)
        r_stage = region(MT * CW)
        xs = sb("xs", [P, MT, D_MODEL], F32, r_x)
        h_hi = [sb(f"h_hi{m}", [P, KT, P], F32R, r_h + 8 * m * HALF) for m in range(MT)]
        h_lo = [sb(f"h_lo{m}", [P, KT, P], F32R, r_h + 8 * m * HALF + 4 * HALF) for m in range(MT)]
        y = [sb(f"y{m}", [P, D_MODEL], F32, r_h + 8 * m * HALF) for m in range(MT)]
        gain = sb("gain", [P, D_MODEL], F32, r_h + 12 * HALF)
        a_hi = sb("a_hi", [P, FT, SEQ], F32R, r_act)
        a_lo = sb("a_lo", [P, FT, SEQ], F32R, r_act + 4 * FT * SEQ)
        at = r_act
        qk = sb("qk", [P, 24, SEQ], F32, at)
        skt = sb("skt", [P, KV_HEADS, SEQ], F32, at + 4 * 24 * SEQ)
        dv = sb("dv", [P, MT, WIDTH], F32, at + 4 * 28 * SEQ)
        sv = sb("sv", [P, MT, KV_HEADS * HD], F32, at + 4 * 36 * SEQ)
        gates = sb("gates", [P, MT, 2 * D_MODEL], F32, at + 4 * 38 * SEQ)
        sc = sb("sc", [P, 2, 2, 3 * P], F32, at + 4 * 70 * SEQ)
        pt = sb("pt", [P, 2, 2, 3 * P], F32, at + 4 * 76 * SEQ)
        assert 82 * SEQ <= 2 * FT * SEQ
        z_hi = sb("z_hi", [P, KT, SEQ], F32R, at)
        z_lo = sb("z_lo", [P, KT, SEQ], F32R, at + 4 * KT * SEQ)
        raw = sb("raw", [P, 4, 4, CW], F32, r_raw)
        w_hi = sb("w_hi", [P, 4, 2, CW], F32R, r_hi)
        w_lo = sb("w_lo", [P, 4, 2, CW], F32R, r_lo)
        stage = sb("stage", [P, MT, CW], F32, r_stage)
        ident = sb("ident", [P, P], F32, region(P))
        dist = sb("dist", [P, 2, 3 * P], F32, region(6 * P))
        junk = sb("junk", [P, CW], BF16, region(CW // 2))
        rows = sb("rows", [P, 2, P], F32, r_act)
        cols = sb("cols", [P, 3 * KT + 1], F32, region(56))
        lamp = sb("lamp", [P, 4, HD], F32, r_act + 8 * P)
        lprod = sb("lprod", [P, 2, HD], F32, r_act + 8 * P + 16 * HD)
        lsum = sb("lsum", [P, 2], F32, region(8))
        lexp = sb("lexp", [P, 2], F32, region(8))
        nlam = sb("nlam", [P, 1], F32, region(8))
        headgain = sb("headgain", [P, 1], F32, region(8))
        sink = sb("sink", [P, SWA_HEADS], F32, region(16))
        nsink = sb("nsink", [P, SWA_HEADS], F32, region(16))
        half = sb("half", [P, 2], F32, region(8))
        ssum = sb("ssum", [P, 2], F32, region(8))
        ssq = sb("ssq", [P, MT, NG], F32, region(8))
        ssx = sb("ssx", [P, MT, NG], F32, region(8))
        sso = sb("sso", [P, HEADS, MT], F32, region(16))
        var = sb("var", [P, ROOTS, MT], F32, region(32))
        root = sb("root", [P, ROOTS, MT], F32, region(32))
        qk_factor = sb("qk_factor", [P, QKV_LOOPS], F32, region(8))
        nmax = sb("nmax", [P, 2, MT, 2], F32, region(8))
        tsink = sb("tsink", [P, 2, MT, 2], F32, region(8))
        esink = sb("esink", [P, 2, MT, 2], F32, region(8))
        sums = sb("sums", [P, 2, MT, 2], F32, region(8))
        rsum = sb("rsum", [P, 2, MT, 2], F32, region(8))
        mixw = sb("mixw", [P, 2, MT], F32, region(8))
        assert place[0] <= nc.sbuf_usable_end
        ctx.enter_context(nc.sbuf_tensor("arena", [P, (place[0] - base) // 4], F32))

        acc = ctx.enter_context(nc.psum_tensor("acc", [P, 2, MT, CW], F32))
        tp = ctx.enter_context(nc.psum_tensor("tp", [P, 4, CW], F32))

        def sem(name):
            return ctx.enter_context(nc.semaphore(name))

        x_in = [sem(f"x_in{q}") for q in range(NG)]
        rows_in = sem("rows_in")
        late_rows_in = sem("late_rows_in")
        small_in = sem("small_in")
        gain_in = sem("gain_in")
        raw_in = [sem(f"raw_in{s}") for s in range(4)]
        odd_in = [sem(f"odd_in{g}") for g in range(2)]
        out_written = sem("out_written")
        consts_made = sem("consts_made")
        gp_step = sem("gp_step")
        hi_ready = sem("hi_ready")
        lo_ready = sem("lo_ready")
        multiplied = sem("multiplied")
        tile0_done = sem("tile0_done")
        acc_free = [sem("acc_free0"), sem("acc_free1")]
        turned = sem("turned")
        scaled = sem("scaled")
        piece_hi = sem("piece_hi")
        piece_out = sem("piece_out")
        squared = sem("squared")
        x_new = sem("x_new")
        x_new_gp = sem("x_new_gp")
        y_scaled = sem("y_scaled")
        var_ready = sem("var_ready")
        root_ready = sem("root_ready")
        cols_turned = sem("cols_turned")
        cols_copied = sem("cols_copied")
        lam_sums = sem("lam_sums")
        lam_exps = sem("lam_exps")
        sig_ready = sem("sig_ready")
        z_ready = sem("z_ready")
        scored = sem("scored")
        score_read = sem("score_read")
        nmax_ready = sem("nmax_ready")
        exp_ready = sem("exp_ready")
        mixed = sem("mixed")
        p_turned = sem("p_turned")
        p_copied = sem("p_copied")
        pv_done = sem("pv_done")
        o_read = sem("o_read")
        o_scaled = sem("o_scaled")
        dve_step = sem("dve_step")

        def last_y(k, m, par=1):
            return 2 * ([U_C] * 2, U_F, [U_H[0] + 2, U_H[1] + 2])[k][par] - 1 + m

        def bank(i):
            return (i + 2) % 4

        w1_in, w1_out = ffn1_w_in[0], ffn1_w_out[0]
        w2_in, w2_out = ffn2_w_in[0], ffn2_w_out[0]
        x_d = x[0].rearrange("(m p) n -> p m n", p=P)
        out_d = out[0].rearrange("(m p) n -> p m n", p=P)
        block = ctx.enter_context(nc.Block())

        @block.sync
        def _(sp):
            def load(b8, j, w, row, tiles, col, width):
                if not (isinstance(b8, int) and 4 * b8 + j < 4):
                    sp.wait_ge(lo_ready, b8 * 8 + (2 * j - 6))
                src = w[row:row + tiles * P, bass.ds(col, width)].rearrange("(k p) n -> p k n", p=P)
                sp.dma_start(raw[:, j % 4, 0:tiles, 0:width], src).then_inc(raw_in[j % 4], 16)

            def chunk(b8, w, col, width=CW):
                for j in range(4):
                    load(b8, j, w, j * 4 * P, 4, col, width)

            def gate_up(b8, w, begun=False):
                def pair(i, width):
                    if not begun or not isinstance(i, int) or i > 0:
                        chunk(b8 + 2 * i, w, i * CW, width)
                    chunk(b8 + 2 * i + 1, w, D_FF + i * CW, width)
                pair(0, CW)
                with sp.Fori(1, PAIRS) as i:
                    pair(i, CW)
                pair(PAIRS, TAIL)

            def hidden_out(b8, w):
                with sp.Fori(0, NG) as n:
                    row = 0
                    for j, tiles in enumerate(OUT_GROUPS):
                        load(b8 + 3 * n, j, w, row * P, tiles, n * CW, CW)
                        row += tiles

            def load_x(q):
                sp.dma_start(xs[:, :, q * CW:(q + 1) * CW], x_d[:, :, q * CW:(q + 1) * CW]).then_inc(x_in[q], 16)
            load_x(0)
            for g in range(2):
                for h, landed in ((0, raw_in[g]), (1, odd_in[g])):
                    row = (4 * g + 2 * h) * P
                    src = w1_in[row:row + 2 * P, 0:CW].rearrange("(k p) n -> p k n", p=P)
                    sp.dma_start(raw[:, g, 2 * h:2 * h + 2, :], src).then_inc(landed, 16)
                load_x(g + 1)
            load(A8, 2, w1_in, 8 * P, 4, 0, CW)
            load_x(3)
            load(A8, 3, w1_in, 12 * P, 4, 0, CW)
            for k, g in enumerate((mix_norm_pre, ffn2_norm_pre)):
                sp.dma_start(rows[k * KT:(k + 1) * KT, 1, :],
                             g[0].rearrange("(t p) -> t p", p=P)).then_inc(late_rows_in, 16)
            sp.dma_start(rows[2 * KT:2 * KT + 1, 1, :], diff_subln[0:1, :]).then_inc(late_rows_in, 16)
            sp.dma_start(lamp[:], diff_lambda.rearrange("a b c -> a (b c)").partition_broadcast(P))\
                .then_inc(small_in, 16)
            sp.dma_start(sink[:], swa_sinks[0:1, :].partition_broadcast(P)).then_inc(small_in, 16)
            gate_up(A8, w1_in, True)
            hidden_out(B8, w1_out)
            dv_col, sq_col = 2 * WIDTH, 3 * WIDTH
            with sp.Fori(0, 2) as i:
                for h in range(2):
                    chunk(C8 + 2 * i + h, w_in[0], i * WIDTH + h * CW)
            for c, col in enumerate([sq_col, sq_col + CW, dv_col, dv_col + CW]):
                chunk(C8 + 4 + c, w_in[0], col)
            with sp.Fori(0, 1 + GATE_CHUNKS) as c:
                chunk(C8 + 8 + c, w_in[0], c * CW + 4 * WIDTH)
            with sp.Fori(0, NG) as n:
                for j in range(4):
                    w = (w_branch_diff, w_branch_swa)[j // 2][0]
                    load(D8 + n, j, w, j % 2 * 4 * P, 4, n * CW, CW)
            with sp.Fori(0, NG) as n:
                chunk(E8 + n, w_out[0], n * CW)
            gate_up(F8, w2_in)
            hidden_out(H8, w2_out)
            before = 2 * DVE_PIECES
            sp.wait_ge(x_new, before + NG)
            sp.dma_start(out_d[:, 0, :], xs[:, 0, :]).then_inc(out_written, 16)
            for q in range(NG):
                sp.wait_ge(x_new, before + NG + q + 1)
                sp.dma_start(out_d[:, 1, q * CW:(q + 1) * CW], xs[:, 1, q * CW:(q + 1) * CW]).then_inc(out_written, 16)
            sp.wait_ge(out_written, 16 * (1 + NG))

        @block.gpsimd
        def _(gp):
            steps = [0]

            def link(ins):
                steps[0] += 1
                ins.then_inc(gp_step, 1)
                gp.wait_ge(gp_step, steps[0])

            link(nc.gpsimd.memset(ident[:], 0.0))
            nc.gpsimd.affine_select(out=ident[:], in_=ident[:], compare_op=ALU.not_equal, fill=1.0, base=0,
                                    pattern=[[-1, P]], channel_multiplier=1).then_inc(consts_made, 1)
            nc.gpsimd.memset(half[:], -0.5).then_inc(consts_made, 1)
            for kind in range(2):
                nc.gpsimd.iota(dist[:, kind, 0:P], pattern=[[-1, P]], base=0, channel_multiplier=1,
                               allow_small_or_imprecise_dtypes=True)
                link(nc.gpsimd.iota(dist[:, kind, P:3 * P], pattern=[[-1, 2 * P]], base=P, channel_multiplier=1,
                                    allow_small_or_imprecise_dtypes=True))
                for lo, n, b in ((0, P, 0), (P, 2 * P, P)):
                    d = dist[:, kind, lo:lo + n]
                    link(nc.gpsimd.affine_select(out=d, in_=d, compare_op=ALU.is_ge, fill=MASKED, base=b,
                                                 pattern=[[-1, n]], channel_multiplier=1))
                    if kind:
                        link(nc.gpsimd.affine_select(out=d, in_=d, compare_op=ALU.is_ge, fill=MASKED,
                                                     base=WINDOW - 1 - b, pattern=[[1, n]],
                                                     channel_multiplier=-1))
            for i, (n, m) in enumerate(ROOT_STEPS):
                gp.wait_ge(var_ready, i + 1)
                if i == 0:
                    gp.wait_ge(consts_made, 2)
                ms = slice(0, MT) if m is None else slice(m, m + 1)
                nc.gpsimd.tensor_tensor(root[:, n, ms], var[:, n, ms], half[:, ms], ALU.pow).then_inc(root_ready, 1)
                if n in R_POST[:2] and m == 1:
                    k = R_POST.index(n)
                    for q, t in PIECES[DVE_PIECES:]:
                        run = [r for r, (rt, q0, q1) in enumerate(Y_RUNS) if rt == t and q0 <= q < q1][0]
                        gp.wait_ge(y_scaled, len(Y_RUNS) * k + run + 1)
                        c = slice(q * CW, (q + 1) * CW)
                        nc.gpsimd.tensor_tensor(xs[:, t, c], xs[:, t, c], y[t][:, c], ALU.add).then_inc(x_new_gp, 1)

        @block.tensor
        def _(pe):
            def chunk(b8, par, lhs, subs, width=CW, before=None, at=0, skew=()):
                def products(j, m):
                    if before and (j, m) in before:
                        before[j, m]()
                    if m == 0:
                        if before and j in before:
                            before[j]()
                        pe.wait_ge(lo_ready, b8 * 8 + (at + j + 1))
                    for t, k in enumerate(subs[j]):
                        first = j == 0 and t == 0
                        last = j == len(subs) - 1 and t == len(subs[j]) - 1
                        s = (at + j) % 4
                        wh, wl = w_hi[:, s, t, 0:width], w_lo[:, s, t, 0:width]
                        xh, xl = lhs(k, m)
                        o = acc[:, par, m, 0:width]
                        nc.tensor.matmul(o, xh, wh, start=first, stop=False)
                        nc.tensor.matmul(o, xh, wl, start=False, stop=False)
                        mm = nc.tensor.matmul(o, xl, wh, start=False, stop=last)
                    if m == 1:
                        mm.then_inc(multiplied, 1)
                    elif j == len(subs) - 1 and j in skew and skew[0] > 0:
                        mm.then_inc(tile0_done, 1)
                order = [(j, m) for j in range(len(subs)) if j not in skew for m in range(MT)]
                run = [(j, m) for m in range(MT) for j in skew]
                if skew and skew[0] == 0:
                    order = run + order
                else:
                    order += run
                for j, m in order:
                    products(j, m)

            def from_h(k, m):
                return h_hi[m][:, k, :], h_lo[m][:, k, :]

            def from_a(k, m):
                return a_hi[:, k, m * P:(m + 1) * P], a_lo[:, k, m * P:(m + 1) * P]

            def from_z(k, m):
                return z_hi[:, k, m * P:(m + 1) * P], z_lo[:, k, m * P:(m + 1) * P]

            def turn(src, b, tiles):
                for t in range(tiles):
                    mm = nc.tensor.transpose(tp[:, b, t * P:(t + 1) * P], src(t), ident[:])
                mm.then_inc(turned, 1)

            def turn_stage(pieces, tiles=4):
                pe.wait_ge(piece_out, pieces)
                for m in range(MT):
                    turn(lambda t: stage[:, m, t * P:(t + 1) * P], m, tiles)

            def boundary(pc, ready, src):
                def piece(i):
                    q, m = PIECES[i]
                    ready(i)
                    if i >= 4:
                        pe.wait_ge(piece_out, pc + i - 3)
                    elif pc:
                        pe.wait_ge(piece_out, pc)
                    turn(lambda t: src(4 * q + t, m), bank(i), 4)

                def have(n):
                    pe.wait_ge(piece_out, pc + n)
                def first_two():
                    piece(0)
                    piece(1)
                if pc:
                    start = {(0, 0): lambda: have(1), (2, 0): lambda: have(2),
                             (3, 0): lambda: piece(2), (0, 1): lambda: (piece(3), have(3))}
                else:
                    start = {(0, 0): lambda: (piece(0), have(1)), (1, 0): lambda: piece(1),
                             (2, 0): lambda: (pe.wait_ge(cols_copied, 1), piece(2), piece(3), have(2)),
                             (0, 1): lambda: have(3)}
                return first_two, {
                        **start,
                        (1, 1): lambda: (piece(4), piece(5)), (2, 1): lambda: have(4),
                        (3, 1): lambda: (piece(6), piece(7)),
                        (4, 0): lambda: have(5), (4, 1): lambda: have(6),
                        (6, 0): lambda: have(7), (6, 1): lambda: have(8)}

            def x_tile(k, m):
                return xs[:, m, k * P:(k + 1) * P]

            def gate_up(b8, pc, uses, hooks):
                def pair(i, width, gate_hooks, skew=()):
                    if not isinstance(i, int) or uses[0] + i > 0:
                        pe.wait_ge(acc_free[0], 2 * (uses[0] + i))
                    chunk(b8 + 2 * i, 0, from_h, FULL_SUBS, width, gate_hooks, skew=skew)
                    if not isinstance(i, int) or uses[1] + i > 0:
                        pe.wait_ge(acc_free[1], 2 * (uses[1] + i))
                    chunk(b8 + 2 * i + 1, 1, from_h, FULL_SUBS, width)

                def turn_last(i):
                    def hook():
                        pe.wait_ge(acc_free[1], 2 * (uses[1] + i))
                        turn_stage(pc + 2 * (i - 1))
                    return hook
                pair(0, CW, hooks, range(SKEW))
                with pe.Fori(1, PAIRS) as i:
                    pair(i, CW, {1: turn_last(i)})
                pair(PAIRS, TAIL, {1: turn_last(PAIRS)})

            def turn_tail(pc, uses):
                def hook():
                    pe.wait_ge(acc_free[1], 2 * (uses[1] + PAIRS + 1))
                    turn_stage(pc + 2 * PAIRS, TAIL // P)
                return hook

            def down(b8, uses, lhs, subs, pieces, turn_last=None, turn_first=None):
                def two(t, hook):
                    for par in range(2):
                        pe.wait_ge(acc_free[par], 2 * (uses[par] + t))
                        late = {len(subs) - (3 if len(subs) > 8 else 2): lambda: pe.wait_ge(piece_out, pieces)}
                        if hook and par == 0:
                            late[2] = hook
                        if turn_first and par and t:
                            late[len(subs) - 2, 1] = turn_first
                        chunk(b8 + (2 * t + par) * (len(subs) // 8), par, lhs, subs, before=late,
                              skew=range(len(subs) - SKEW, len(subs)) if par and t else ())
                two(0, turn_last)
                two(1, None)

            def turn_rows(group, n, b):
                nc.tensor.transpose(tp[:, b, 0:n], rows[0:n, group, :], ident[0:n, 0:n]).then_inc(cols_turned, 1)

            def turn_late_rows():
                pe.wait_ge(late_rows_in, 16 * 3)
                turn_rows(1, 2 * KT + 1, 2)
            pe.wait_ge(rows_in, 16)
            pe.wait_ge(consts_made, 1)
            turn_rows(0, KT, 1)

            hooks = boundary(PC_START, lambda i: pe.wait_ge(x_in[PIECES[i][0]], 16), x_tile)[1]
            hooks[7] = turn_late_rows
            gate_up(A8, PC_A, [0, 0], hooks)

            def updated(k):
                def ready(i):
                    if i < DVE_PIECES:
                        pe.wait_ge(x_new, DVE_PIECES * k + i + 1)
                    else:
                        pe.wait_ge(x_new_gp, (len(PIECES) - DVE_PIECES) * k + i - DVE_PIECES + 1)
                return ready
            turn_first, hooks = boundary(PC_BC, updated(0), x_tile)
            down(B8, [U_B, U_B], from_a, HIDDEN_SUBS, PC_BC, turn_tail(PC_A, [0, 0]), turn_first)

            def turn_qk(c, par, i):
                def hook():
                    pe.wait_ge(acc_free[par], 2 * (U_C + i + 1))
                    turn_stage(PC_QK + 2 * c)
                return hook

            def qk_pair(i, first_hooks):
                for par in range(2):
                    pe.wait_ge(acc_free[par], 2 * (U_C + i))
                    chunk(C8 + 2 * i + par, par, from_h, FULL_SUBS,
                          before={2: turn_qk(2 * i, 0, i)} if par else first_hooks,
                          skew=range(SKEW) if isinstance(i, int) and i + par == 0 else ())

            qk_pair(0, hooks)
            with pe.Fori(1, QKV_LOOPS) as i:
                qk_pair(i, {2: turn_qk(2 * i - 1, 1, i - 1)})
            for c in range(6, QKV_CHUNKS - 1):
                pe.wait_ge(acc_free[c % 2], 2 * (U_C + c // 2))
                chunk(C8 + c, c % 2, from_h, FULL_SUBS, before={2: turn_qk(5, 1, 2)} if c == 6 else None)

            def scores(u):
                qt = u if u < HEADS else 16 + u - HEADS
                if u:
                    pe.wait_ge(score_read, u)
                if u in (0, SK_UNIT + 1):
                    pe.wait_ge(piece_out, PC_SK if u == 0 else PC_O)
                for m in range(MT):
                    for c in range(2):
                        r = slice(c * HD, (c + 1) * HD)
                        kt = qk[r, HEADS + u, :] if u < HEADS else skt[r, (u - HEADS) // 2, :]
                        mm = nc.tensor.matmul(tp[:, 2 + c, m * P:P + 2 * m * P], qk[r, qt, m * P:(m + 1) * P],
                                              kt[:, 0:(m + 1) * P], start=True, stop=True)
                mm.then_inc(scored, 1)

            def turn_p(u):
                pe.wait_ge(mixed, u + 1)
                if u:
                    pe.wait_ge(o_read, u)
                for c in range(1 if u < HEADS else 2):
                    for b in range(3):
                        mm = nc.tensor.transpose(tp[:, c, b * P:(b + 1) * P], sc[:, u % 2, c, b * P:(b + 1) * P],
                                                 ident[:])
                mm.then_inc(p_turned, 1)

            def pv(u):
                pe.wait_ge(p_copied, u + 1)
                if u == 0:
                    pe.wait_ge(acc_free[1], 2 * (U_C + 4))
                for c in range(1 if u < HEADS else 2):
                    n = P if u < HEADS else HD
                    for m in range(MT):
                        o = tp[:, m, 3 * P + c * HD:3 * P + c * HD + n]
                        for k in range(m + 1):
                            v = dv[:, k, u * P:(u + 1) * P] if u < HEADS else \
                                sv[:, k, (u - HEADS) // 2 * HD:(u - HEADS) // 2 * HD + HD]
                            b = m + k
                            mm = nc.tensor.matmul(o, pt[:, u % 2, c, b * P:(b + 1) * P], v,
                                                  start=(k == 0), stop=(k == m))
                mm.then_inc(pv_done, 1)

            hooks = {}
            for u in range(UNITS):
                hooks.setdefault(4 * u, []).append(lambda u=u: scores(u))
            for u in range(UNITS):
                hooks.setdefault(4 * u + 4, []).append(lambda u=u: turn_p(u))
                hooks.setdefault(4 * u + 6, []).append(lambda u=u: pv(u))

            def turn_sk():
                pe.wait_ge(acc_free[0], 2 * (U_C + QKV_CHUNKS // 2 + 1))
                pe.wait_ge(score_read, SK_UNIT + 1)
                for m in range(MT):
                    turn(lambda t: stage[:, m, t * P:(t + 1) * P], 2 + m, 4)
            hooks[4 * SK_UNIT + 2].insert(0, turn_sk)

            def o_tile(k, m):
                return qk[:, k if k < HEADS else 16 + k - HEADS, m * P:(m + 1) * P]

            def turn_o(q):
                def hook():
                    if q == 0:
                        pe.wait_ge(o_scaled, HEADS)
                        pe.wait_ge(score_read, UNITS)
                    elif q == 1:
                        pe.wait_ge(o_read, UNITS)
                    for m in range(MT):
                        if q >= 2:
                            pe.wait_ge(piece_out, PC_O + 2 * q + m - 3)
                        turn(lambda t: o_tile(4 * q + t, m), bank(2 * q + m), 4)
                return hook
            hooks.setdefault(O_TURN, []).append(turn_o(0))
            hooks.setdefault(O_TURN + 2, []).append(turn_o(1))
            for g in range(ATT_CHUNKS):
                c = QKV_CHUNKS - 1 + g
                pe.wait_ge(acc_free[c % 2], 2 * (U_C + c // 2))
                chunk(C8 + c, c % 2, from_h, FULL_SUBS, before=chunk_hooks(hooks, g),
                      skew=range(SUBS - SKEW, SUBS) if g == ATT_CHUNKS - 1 else ())

            def branch(n, first, second, skew=()):
                for par, hk in ((0, first), (1, second)):
                    if not (skew and par == 0):
                        pe.wait_ge(acc_free[par], 2 * (U_D[par] + n))
                    chunk(D8 + n, par, from_h, FULL_SUBS[4 * par:4 * par + 4], before=hk, at=4 * par,
                          skew=() if par else skew)

            def turn_z(n):
                def hook():
                    pe.wait_ge(z_ready, 2 * n)
                    turn_stage(PC_D + 2 * (n - 1))
                return hook

            def have(q):
                pe.wait_ge(piece_out, PC_O + 2 * (q + 1))
            branch(0, {0: lambda: (pe.wait_ge(acc_free[0], 2 * U_D[0] - 1), have(0), turn_o(2)()),
                       2: lambda: (have(1), turn_o(3)()), (0, 1): lambda: pe.wait_ge(acc_free[0], 2 * U_D[0])},
                   {0: lambda: have(2), 2: lambda: have(3)}, range(4))
            with pe.Fori(1, NG) as n:
                branch(n, {2: turn_z(n)}, None)

            turn_first, hooks = boundary(PC_EF, updated(1), x_tile)
            down(E8, U_E, from_z, FULL_SUBS, PC_EF, turn_z(NG), turn_first)
            gate_up(F8, PC_F, U_F, hooks)
            down(H8, U_H, from_a, HIDDEN_SUBS, PC_F + 2 * (PAIRS + 1), turn_tail(PC_F, U_F))

        @block.scalar
        def _(act):
            def split(b8, j):
                s = j + LEAD
                if isinstance(b8, int) and 8 * b8 + s >= TOTAL_SUBS:
                    return
                g = s // 2
                if s % 2 == 0:
                    act.wait_ge(raw_in[g % 4], b8 * 16 + 16 * (g // 4 + 1))
                elif isinstance(b8, int) and 8 * b8 + s in (1, 3):
                    act.wait_ge(odd_in[g], 16)
                if not (isinstance(b8, int) and 8 * b8 + s < 4):
                    act.wait_ge(multiplied, b8 * 8 + (s - 3))
                nc.scalar.activation(w_hi[:, s % 4], raw[:, g % 4, s % 2 * 2:s % 2 * 2 + 2], ACT.Copy)\
                    .then_inc(hi_ready, 1)

            def steps(b8, n, before=None):
                for j in range(n):
                    if before and j in before:
                        before[j]()
                    split(b8, j)

            def await_turned(pc):
                return lambda: act.wait_ge(turned, pc + 2)

            def plain_hi(dst, tiles=4):
                for m in range(MT):
                    nc.scalar.activation(dst(m), tp[:, m, 0:tiles * P], ACT.Copy).then_inc(piece_hi, 1)

            def piece_parts(sc0):
                def take(*pieces):
                    for i in pieces:
                        q, m = PIECES[i]
                        act.wait_ge(scaled, sc0 + i + 1)
                        nc.scalar.activation(h_hi[m][:, 4 * q:4 * q + 4, :], stage[:, i % 2, :], ACT.Copy)\
                            .then_inc(piece_hi, 1)
                return take

            def boundary(sc0, k):
                take = piece_parts(sc0)

                def scale_y():
                    for m, q0, q1 in Y_RUNS if k else ():
                        act.wait_ge(root_ready, root_count(R_POST[k - 1], m))
                        par = 1 if q1 == NG else 0
                        act.wait_ge(acc_free[par], last_y(k - 1, m, par))
                        c = slice(q0 * CW, q1 * CW)
                        nc.scalar.activation(y[m][:, c], y[m][:, c], ACT.Copy,
                                             scale=root[:, R_POST[k - 1], m:m + 1]).then_inc(y_scaled, 1)
                return {1: lambda: (scale_y(), take(2, 3)), 2: lambda: take(4, 5),
                        4: lambda: take(6, 7), 6: square_x(k)}

            def square(n, src, total):
                if not (isinstance(n, int) and n == 0):
                    act.wait_ge(squared, n)
                nc.scalar.activation(junk[:, 0:src.shape[-1]], src, ACT.Square, accum_out=total)\
                    .then_inc(squared, 1)

            def square_x(k):
                def hook():
                    for m in range(MT):
                        for q in range(NG):
                            if k == 0:
                                act.wait_ge(x_in[q], 16)
                            square(Q_X[k] + m * NG + q, xs[:, m, q * CW:(q + 1) * CW], ssx[:, m, q:q + 1])
                return hook

            def gate_up(b8, pc, uses, k, hooks):
                def pair(i, width, gate_hooks):
                    steps(b8 + 2 * i, 8, gate_hooks)
                    if isinstance(i, int) and i == 0:
                        act.wait_ge(root_ready, root_count(R_PRE[k]))
                    act.wait_ge(turned, pc + 2 * i)
                    act.wait_ge(multiplied, (b8 + 2 * i) * 8 + 8)
                    for m in range(MT):
                        nc.scalar.activation(stage[:, m, 0:width], acc[:, 0, m, 0:width], ACT.Silu,
                                             scale=root[:, R_PRE[k], m:m + 1]).then_inc(acc_free[0], 1)
                    steps(b8 + 2 * i + 1, 8)

                def last_hi(i):
                    return {4: await_turned(pc + 2 * (i - 1)),
                            5: lambda: plain_hi(lambda m: a_hi[:, bass.ds(4 * (i - 1), 4), m * P:(m + 1) * P])}
                pair(0, CW, hooks)
                with act.Fori(1, PAIRS) as i:
                    pair(i, CW, last_hi(i))
                pair(PAIRS, TAIL, last_hi(PAIRS))

            def tail_hi(pc):
                n = TAIL // P
                return {4: await_turned(pc + 2 * PAIRS),
                        5: lambda: plain_hi(lambda m: a_hi[:, 4 * PAIRS:4 * PAIRS + n, m * P:(m + 1) * P], n)}

            def down(b8, units, k, g_d, after, first=None):
                act.wait_ge(multiplied, 8 * b8)
                act.dma_start(gain[:], g_d[0:1, :].partition_broadcast(P)).then_inc(gain_in, 16)

                def square_y(n, m):
                    square(Q_Y[k] + 2 * n + m, acc[:, n % 2, m, :], ssq[:, m, n:n + 1])
                subs = 8 * units
                for n in range(NG - 1):
                    n8 = b8 + n * units
                    steps(n8, subs, first if n == 0 else None)
                    act.wait_ge(multiplied, (n8 + units) * 8)
                    for m in range(MT):
                        square_y(n, m)

                n8 = b8 + (NG - 1) * units

                def tile0():
                    act.wait_ge(tile0_done, (1, 3, 4)[k])
                    square_y(NG - 1, 0)

                def tile1():
                    act.wait_ge(multiplied, (n8 + units) * 8)
                    square_y(NG - 1, 1)
                hooks = {subs - SKEW + 1: tile0}
                if after is not None:
                    hooks[subs - 1] = lambda: piece_parts(after)(0, 1)
                steps(n8, subs, hooks)
                tile1()

            act.dma_start(rows[0:KT, 0, :], ffn1_norm_pre[0].rearrange("(t p) -> t p", p=P)).then_inc(rows_in, 16)
            piece_parts(SC_START)(0)
            for j in range(-LEAD, 0):
                split(0, j)
            piece_parts(SC_START)(1)

            gate_up(A8, PC_A, [0, 0], 0, boundary(SC_START, 0))
            down(B8, 3, 0, ffn1_norm_post, SC_BC, tail_hi(PC_A))

            def to_stage(par, c):
                act.wait_ge(turned, PC_QK + 2 * c)
                act.wait_ge(multiplied, (C8 + c) * 8 + 8)
                for m in range(MT):
                    nc.scalar.activation(stage[:, m, :], acc[:, par, m, :], ACT.Copy,
                                         scale=root[:, R_PRE[1], m:m + 1]).then_inc(acc_free[par], 1)

            def qk_pair(i, hooks):
                for par in range(2):
                    steps(C8 + 2 * i + par, 8, None if par else hooks)
                    if isinstance(i, int) and i == 0 and par == 0:
                        act.wait_ge(root_ready, root_count(R_PRE[1]))
                    to_stage(par, 2 * i + par)
            qk_pair(0, boundary(SC_BC, 1))
            with act.Fori(1, QKV_LOOPS) as i:
                qk_pair(i, None)
            act.wait_ge(lam_sums, 1)
            nc.scalar.activation(lexp[:], lsum[:], ACT.Exp).then_inc(lam_exps, 1)
            rs = R_PRE[1]
            for c in (6, 7):
                steps(C8 + c, 8)
                act.wait_ge(multiplied, (C8 + c) * 8 + 8)
                for m in range(MT):
                    nc.scalar.activation(dv[:, m, (c - 6) * CW:(c - 5) * CW], acc[:, c % 2, m, :], ACT.Copy,
                                         scale=root[:, rs, m:m + 1]).then_inc(acc_free[c % 2], 1)
            def exps(u):
                act.wait_ge(nmax_ready, u + 1)
                b = u % 2
                for c in range(2):
                    for m in range(MT):
                        s = sc[:, b, c, m * P:P + 2 * m * P]
                        ins = nc.scalar.activation(s, s, ACT.Exp, bias=nmax[:, b, m, c:c + 1],
                                                   accum_out=sums[:, b, m, c:c + 1])
                if u >= HEADS:
                    ins = nc.scalar.activation(esink[:, b], tsink[:, b], ACT.Exp)
                ins.then_inc(exp_ready, 1)

            def copy_p(u):
                act.wait_ge(p_turned, u + 1)
                if u >= 2:
                    act.wait_ge(pv_done, u - 1)
                n = 1 if u < HEADS else 2
                nc.scalar.activation(pt[:, u % 2, 0:n], tp[:, 0:n, 0:3 * P], ACT.Copy).then_inc(p_copied, 1)

            def square_o(u):
                act.wait_ge(o_read, u + 1)
                for m in range(MT):
                    square(Q_O + 2 * u + m, qk[:, u, m * P:(m + 1) * P], sso[:, u, m:m + 1])

            hooks = {}
            for u in range(UNITS):
                hooks.setdefault(4 * u + 1, []).append(lambda u=u: exps(u))
                hooks.setdefault(4 * u + 5, []).append(lambda u=u: copy_p(u))
                if u < HEADS:
                    hooks.setdefault(4 * u + 9, []).append(lambda u=u: square_o(u))

            def o_hi(q):
                def hook():
                    act.wait_ge(multiplied, 8 * D8 - 4 if q < 2 else 8 * D8)
                    for m in range(MT):
                        if q >= 2:
                            act.wait_ge(turned, PC_O + 2 * q + m + 1)
                            src = tp[:, bank(2 * q + m), :]
                        else:
                            act.wait_ge(scaled, SC_O + 2 * q + m + 1)
                            src = stage[:, m, :]
                        nc.scalar.activation(h_hi[m][:, 4 * q:4 * q + 4, :], src, ACT.Copy).then_inc(piece_hi, 1)
                return hook
            hooks.setdefault(O_TURN + 1, []).append(o_hi(0))
            hooks.setdefault(O_TURN + 3, []).append(o_hi(1))
            KW = KV_HEADS * HD

            def take_gates(g, m):
                par = (QKV_CHUNKS - 1 + g) % 2
                nc.scalar.activation(gates[:, m, (g - 1) * CW:g * CW], acc[:, par, m, :], ACT.Copy,
                                     scale=root[:, rs, m:m + 1]).then_inc(acc_free[par], 1)
            for g in range(ATT_CHUNKS):
                c = QKV_CHUNKS - 1 + g
                if g == ATT_CHUNKS - 1:
                    hooks[8 * g + 5].insert(0, lambda: (act.wait_ge(tile0_done, 2), take_gates(ATT_CHUNKS - 1, 0)))
                steps(C8 + c, 8, chunk_hooks(hooks, g))
                act.wait_ge(multiplied, (C8 + c) * 8 + 8)
                for m in range(MT):
                    if g:
                        if g < ATT_CHUNKS - 1 or m:
                            take_gates(g, m)
                        continue
                    dup = stage[:, m, :].rearrange("p (h two d) -> p h two d", two=2, d=HD)
                    for two in range(2):
                        nc.scalar.activation(dup[:, :, two, :], acc[:, 0, m, 0:KW].rearrange("p (h d) -> p h d", d=HD),
                                             ACT.Copy, scale=root[:, rs, m:m + 1])
                    nc.scalar.activation(sv[:, m, :], acc[:, 0, m, KW:2 * KW], ACT.Copy,
                                         scale=root[:, rs, m:m + 1]).then_inc(acc_free[0], 1)

            def sigmoids(n):
                def hook():
                    for m in range(MT):
                        for side in range(2):
                            g = gates[:, m, bass.ds(side * D_MODEL + n * CW, CW)]
                            nc.scalar.activation(g, g, ACT.Sigmoid).then_inc(sig_ready, 1)
                return hook

            def z_piece_hi(n):
                plain_hi(lambda m: z_hi[:, bass.ds(4 * (n - 1), 4), m * P:(m + 1) * P])
            act.wait_ge(acc_free[0], 2 * U_D[0])
            act.wait_ge(acc_free[1], 2 * U_D[1])
            steps(D8, 8, {1: o_hi(2), 3: o_hi(3), 4: sigmoids(0)})
            with act.Fori(1, NG) as n:
                steps(D8 + n, 8, {2: sigmoids(n), 5: await_turned(PC_D + 2 * (n - 1)),
                                  6: lambda: z_piece_hi(n)})

            down(E8, 1, 1, mix_norm_post, SC_EF, {4: await_turned(PC_D + 2 * (NG - 1)), 5: lambda: z_piece_hi(NG)})
            gate_up(F8, PC_F, U_F, 2, boundary(SC_EF, 2))
            down(H8, 3, 2, ffn2_norm_post, None, tail_hi(PC_F))

        @block.vector
        def _(dve):
            chain = [0]

            def link(ins):
                chain[0] += 1
                ins.then_inc(dve_step, 1)
                dve.wait_ge(dve_step, chain[0])

            def split(b8, j):
                s = j + LEAD
                if isinstance(b8, int) and 8 * b8 + s >= TOTAL_SUBS:
                    return
                g = s // 2
                dve.wait_ge(hi_ready, b8 * 8 + (s + 1))
                nc.vector.tensor_tensor(w_lo[:, s % 4], raw[:, g % 4, s % 2 * 2:s % 2 * 2 + 2],
                                        w_hi[:, s % 4].bitcast(F32), ALU.subtract).then_inc(lo_ready, 1)

            def steps(b8, n, before=None):
                for j in range(n):
                    if before and j in before:
                        before[j]()
                    split(b8, j)

            def plain_lo(pc, skip, hi, lo, tiles=4):
                for m in range(MT):
                    dve.wait_ge(piece_hi, pc - skip + m + 1)
                    nc.vector.tensor_tensor(lo(m), tp[:, m, 0:tiles * P].rearrange("p (t n) -> p t n", n=P),
                                            hi(m).bitcast(F32), ALU.subtract).then_inc(piece_out, 1)

            def pieces_of(pc, skip, order, gains):
                def scale(*pieces):
                    for i in pieces:
                        q, m = order[i]
                        if gains(q) is None:
                            continue
                        dve.wait_ge(turned, pc + i + 1)
                        if i >= 2:
                            dve.wait_ge(piece_out, pc + i - 1)
                        nc.vector.tensor_tensor(stage[:, i % 2, :].rearrange("p (t n) -> p t n", n=P),
                                                tp[:, bank(i), :].rearrange("p (t n) -> p t n", n=P), gains(q),
                                                ALU.mult).then_inc(scaled, 1)

                def lo(*pieces):
                    for i in pieces:
                        q, m = order[i]
                        dve.wait_ge(piece_hi, pc - skip + i + 1)
                        src = stage[:, i % 2, :] if gains(q) is not None else tp[:, bank(i), :]
                        nc.vector.tensor_tensor(h_lo[m][:, 4 * q:4 * q + 4, :], src.rearrange("p (t n) -> p t n", n=P),
                                                h_hi[m][:, 4 * q:4 * q + 4, :].bitcast(F32),
                                                ALU.subtract).then_inc(piece_out, 1)
                return scale, lo

            def boundary(k):
                scale, lo = pieces_of(PC_PRE[k], SKIP_PRE[k], PIECES, pre_gain(k))

                return {1: lambda: (scale(2), lo(2), scale(3), lo(3)), 2: lambda: (scale(4, 5), lo(4, 5)),
                        4: lambda: (scale(6, 7), lo(6, 7)), 7: pre_norm(k)}

            def pre_gain(k):
                return lambda q: cols[:, k * KT + 4 * q:k * KT + 4 * q + 4].unsqueeze(2).to_broadcast([P, 4, P])

            def variance(n, total, width, factor=1.0, ms=slice(0, MT)):
                nc.vector.tensor_scalar(var[:, n, ms], total, 1.0 / (width * factor ** 2), EPS / factor ** 2,
                                        ALU.mult, ALU.add).then_inc(var_ready, 1)

            def pre_norm(k):
                def hook():
                    dve.wait_ge(squared, Q_X[k] + 8)
                    link(nc.vector.tensor_reduce(ssum[:], ssx[:], AX.X, ALU.add))
                    variance(R_PRE[k], ssum[:], D_MODEL)
                return hook

            def residual(k):
                def update(*pieces):
                    for i in pieces:
                        q, m = (i % NG, i // NG) if k == 2 else PIECES[i]
                        dve.wait_ge(root_ready, root_count(R_POST[k], m))
                        dve.wait_ge(acc_free[1], last_y(k, m))
                        c = slice(q * CW, (q + 1) * CW)
                        nc.vector.scalar_tensor_tensor(out=xs[:, m, c], in0=y[m][:, c],
                                                       scalar=root[:, R_POST[k], m:m + 1], in1=xs[:, m, c],
                                                       op0=ALU.mult, op1=ALU.add).then_inc(x_new, 1)
                return update

            def gate_up(b8, pc, skip, uses, k, hooks):
                def pair(i, width, gate_hooks):
                    steps(b8 + 2 * i, 8, gate_hooks)
                    steps(b8 + 2 * i + 1, 8)
                    dve.wait_ge(multiplied, (b8 + 2 * i) * 8 + 16)
                    dve.wait_ge(acc_free[0], 2 * (uses[0] + i + 1))
                    for m in range(MT):
                        nc.vector.scalar_tensor_tensor(out=stage[:, m, 0:width], in0=acc[:, 1, m, 0:width],
                                                       scalar=root[:, R_PRE[k], m:m + 1],
                                                       in1=stage[:, m, 0:width],
                                                       op0=ALU.mult, op1=ALU.mult).then_inc(acc_free[1], 1)

                def last_lo(i):
                    return lambda: plain_lo(pc + 2 * (i - 1), skip,
                                            lambda m: a_hi[:, bass.ds(4 * (i - 1), 4), m * P:(m + 1) * P],
                                            lambda m: a_lo[:, bass.ds(4 * (i - 1), 4), m * P:(m + 1) * P])
                pair(0, CW, hooks)
                with dve.Fori(1, PAIRS) as i:
                    pair(i, CW, {4: last_lo(i)})
                pair(PAIRS, TAIL, {4: last_lo(PAIRS)})

            def tail_lo(pc, skip):
                n = TAIL // P
                return {5: lambda: plain_lo(pc + 2 * PAIRS, skip,
                                            lambda m: a_hi[:, 4 * PAIRS:4 * PAIRS + n, m * P:(m + 1) * P],
                                            lambda m: a_lo[:, 4 * PAIRS:4 * PAIRS + n, m * P:(m + 1) * P], n)}

            def down(b8, units, k, factor, first=None):
                def take_y(n, m):
                    dve.wait_ge(squared, Q_Y[k] + 2 * n + m + 1)
                    nc.vector.tensor_tensor(y[m][:, n * CW:(n + 1) * CW], acc[:, n % 2, m, :],
                                            gain[:, n * CW:(n + 1) * CW], ALU.mult).then_inc(acc_free[n % 2], 1)

                def post_var(m):
                    dve.wait_ge(squared, Q_Y[k] + 2 * (NG - 1) + m + 1)
                    link(nc.vector.tensor_reduce(ssum[:, m:m + 1], ssq[:, m, :], AX.X, ALU.add))
                    variance(R_POST[k], ssum[:, m:m + 1], D_MODEL, factor, slice(m, m + 1))
                subs = 8 * units
                dve.wait_ge(gain_in, 16 * (k + 1))
                for n in range(NG - 1):
                    steps(b8 + n * units, subs, first if n == 0 else None)
                    for m in range(MT):
                        take_y(n, m)
                update = residual(k)
                n, n8 = NG - 1, b8 + (NG - 1) * units
                at = subs - SKEW + 1
                if k == 2:
                    steps(n8, subs, {at: lambda: (post_var(0), take_y(n, 0), update(0, 1, 2, 3))})
                    post_var(1)
                    take_y(n, 1)
                    update(4, 5, 6, 7)
                    return
                scale, lo = pieces_of(PC_PRE[k + 1], SKIP_PRE[k + 1], PIECES, pre_gain(k + 1))
                steps(n8, subs, {at: lambda: (post_var(0), take_y(n, 0), update(*range(DVE_PIECES))),
                                 at + 1: lambda: (scale(0, 1), lo(0)),
                                 at + 2: lambda: (lo(1), post_var(1))})
                take_y(n, 1)

            dve.wait_ge(cols_turned, 1)
            nc.vector.tensor_copy(cols[:, 0:KT], tp[:, 1, 0:KT]).then_inc(cols_copied, 1)
            dve.wait_ge(cols_copied, 1)

            def late_cols():
                dve.wait_ge(cols_turned, 2)
                nc.vector.tensor_copy(cols[:, KT:3 * KT + 1], tp[:, 2, 0:2 * KT + 1]).then_inc(cols_copied, 1)
                dve.wait_ge(cols_copied, 2)
                nc.vector.tensor_scalar(headgain[:], cols[:, 3 * KT:3 * KT + 1], 1.0 - LAM_INIT, None, ALU.mult)
            scale, lo = pieces_of(PC_START, 0, PIECES, pre_gain(0))
            scale(0)
            lo(0)
            for j in range(-LEAD, 0):
                split(0, j)
            scale(1)
            lo(1)

            def lambda_sums():
                dve.wait_ge(small_in, 16 * 2)
                nc.vector.tensor_tensor(lprod[:, 0, :], lamp[:, 0, :], lamp[:, 1, :], ALU.mult)
                link(nc.vector.tensor_tensor(lprod[:, 1, :], lamp[:, 2, :], lamp[:, 3, :], ALU.mult))
                nc.vector.tensor_reduce(lsum[:], lprod[:], AX.X, ALU.add).then_inc(lam_sums, 1)
                link(nc.vector.tensor_scalar(nsink[:], sink[:], -1.0, None, ALU.mult))

            hooks = boundary(0)
            hooks[6] = lambda_sums
            norm_hook = hooks[7]
            hooks[7] = lambda: (norm_hook(), late_cols())
            gate_up(A8, PC_A, 0, [0, 0], 0, hooks)
            down(B8, 3, 0, 0.5, tail_lo(PC_A, 0))

            hooks = boundary(1)

            for i in range(QKV_LOOPS):
                ins = nc.vector.memset(qk_factor[:, i:i + 1], 1.0 if i == 1 else HD ** -0.5)
            link(ins)

            def take_qk(c, i):
                def hook():
                    for m in range(MT):
                        dve.wait_ge(turned, PC_QK + 2 * c + m + 1)
                        nc.vector.tensor_scalar(qk[:, bass.ds(4 * c, 4), m * P:(m + 1) * P],
                                                tp[:, m, :].rearrange("p (t n) -> p t n", n=P),
                                                qk_factor[:, bass.ds(i, 1)], None, ALU.mult).then_inc(piece_out, 1)
                return hook

            def qk_pair(i, first_hooks):
                steps(C8 + 2 * i, 8, first_hooks)
                steps(C8 + 2 * i + 1, 8, {4: take_qk(2 * i, i)})
            qk_pair(0, hooks)
            with dve.Fori(1, QKV_LOOPS) as i:
                qk_pair(i, {4: take_qk(2 * i - 1, i - 1)})
            steps(C8 + 6, 8, {4: take_qk(5, 2)})
            dve.wait_ge(lam_exps, 1)
            link(nc.vector.tensor_tensor(nlam[:], lexp[:, 1:2], lexp[:, 0:1], ALU.subtract))
            link(nc.vector.tensor_scalar(nlam[:], nlam[:], -LAM_INIT, None, ALU.add))
            steps(C8 + 7, 8)

            def scores_read(u):
                b = u % 2
                dve.wait_ge(scored, u + 1)
                if u >= 2:
                    dve.wait_ge(p_turned, u - 1)
                if u < HEADS:
                    ins = nc.vector.scalar_tensor_tensor(
                        out=sc[:, b], in0=dist[:, 0:1, :].to_broadcast([P, 2, 3 * P]), scalar=-head_slope(HEADS, u),
                        in1=tp[:, 2:4, 0:3 * P], op0=ALU.mult, op1=ALU.add)
                else:
                    for c in range(2):
                        ins = nc.vector.scalar_tensor_tensor(
                            out=sc[:, b, c], in0=dist[:, 1, :],
                            scalar=-head_slope(SWA_HEADS, 2 * (u - HEADS) + c),
                            in1=tp[:, 2 + c, 0:3 * P], op0=ALU.mult, op1=ALU.add)
                ins.then_inc(score_read, 1)
                dve.wait_ge(score_read, u + 1)
                for m in range(MT):
                    ins = nc.vector.tensor_reduce(nmax[:, b, m, :], sc[:, b, :, m * P:P + 2 * m * P], AX.X,
                                                  ALU.max, negate=True)
                if u >= HEADS:
                    link(ins)
                    h = 2 * (u - HEADS)
                    link(nc.vector.tensor_tensor(nmax[:, b], nmax[:, b],
                                                 nsink[:, h:h + 2].unsqueeze(1).to_broadcast([P, MT, 2]), ALU.min))
                    ins = nc.vector.tensor_tensor(tsink[:, b], nmax[:, b],
                                                  sink[:, h:h + 2].unsqueeze(1).to_broadcast([P, MT, 2]), ALU.add)
                ins.then_inc(nmax_ready, 1)

            def mix(u):
                b = u % 2
                dve.wait_ge(exp_ready, u + 1)
                if u < HEADS:
                    link(nc.vector.reciprocal(rsum[:, b], sums[:, b]))
                    link(nc.vector.scalar_tensor_tensor(out=mixw[:, b], in0=sums[:, b, :, 0], scalar=nlam[:],
                                                        in1=rsum[:, b, :, 1], op0=ALU.mult, op1=ALU.mult))
                    for m in range(MT):
                        r = slice(m * P, P + 2 * m * P)
                        ins = nc.vector.scalar_tensor_tensor(out=sc[:, b, 0, r], in0=sc[:, b, 1, r],
                                                             scalar=mixw[:, b, m:m + 1], in1=sc[:, b, 0, r],
                                                             op0=ALU.mult, op1=ALU.add)
                else:
                    link(nc.vector.tensor_tensor(sums[:, b], sums[:, b], esink[:, b], ALU.add))
                    ins = nc.vector.reciprocal(rsum[:, b], sums[:, b])
                ins.then_inc(mixed, 1)

            def take_o(u):
                b = u % 2
                dve.wait_ge(pv_done, u + 1)
                dve.wait_ge(mixed, u + 1)
                if u < HEADS:
                    ins = nc.vector.tensor_tensor(qk[:, u, :].rearrange("p (m n) -> p m n", n=P),
                                                  tp[:, 0:2, 3 * P:4 * P],
                                                  rsum[:, b, :, 0:1].to_broadcast([P, MT, P]), ALU.mult)
                else:
                    ins = nc.vector.tensor_tensor(
                        qk[:, 16 + u - HEADS, :].rearrange("p (m c n) -> p m c n", c=2, n=HD),
                        tp[:, 0:2, 3 * P:4 * P].rearrange("p m (c n) -> p m c n", n=HD),
                        rsum[:, b].unsqueeze(3).to_broadcast([P, MT, 2, HD]), ALU.mult)
                ins.then_inc(o_read, 1)

            def head_var(u):
                dve.wait_ge(squared, Q_O + 2 * u + 2)
                variance(R_HEAD + u, sso[:, u, :], 2 * HD)

            def head_scale(u):
                dve.wait_ge(root_ready, root_count(R_HEAD + u))
                dve.wait_ge(o_read, u + 1)
                o = qk[:, u, :].rearrange("p (m n) -> p m n", n=P)
                nc.vector.tensor_tensor(o, o, root[:, R_HEAD + u, :].unsqueeze(2).to_broadcast([P, MT, P]),
                                        ALU.mult).then_inc(o_scaled, 1)

            def take_sk():
                for m in range(MT):
                    dve.wait_ge(turned, PC_SK + m + 1)
                    nc.vector.tensor_copy(skt[:, :, m * P:(m + 1) * P],
                                          tp[:, 2 + m, :].rearrange("p (t n) -> p t n", n=P)).then_inc(piece_out, 1)

            hooks = {}
            for u in range(UNITS):
                hooks.setdefault(4 * u + 1, []).append(lambda u=u: scores_read(u))
                hooks.setdefault(4 * u + 3, []).append(lambda u=u: mix(u))
                hooks.setdefault(4 * u + 7, []).append(lambda u=u: take_o(u))
                if u < HEADS:
                    hooks.setdefault(4 * u + 10, []).append(lambda u=u: head_var(u))
                    hooks.setdefault(4 * u + 12, []).append(lambda u=u: head_scale(u))
            hooks[4 * SK_UNIT + 3].insert(0, take_sk)

            def head_gain(q):
                return headgain[:, 0:1].unsqueeze(2).to_broadcast([P, 4, P]) if q < 2 else None
            scale_o, lo_o = pieces_of(PC_O, NO_SPLIT, [(i // 2, i % 2) for i in range(8)], head_gain)

            def o_quarters(q):
                scale_o(2 * q, 2 * q + 1)
                lo_o(2 * q, 2 * q + 1)
            hooks.setdefault(O_TURN + 1, []).append(lambda: o_quarters(0))
            hooks.setdefault(O_TURN + 3, []).append(lambda: o_quarters(1))
            for g in range(ATT_CHUNKS):
                steps(G8 - 1 + g, 8, chunk_hooks(hooks, g))

            def gate_side(side, n):
                dve.wait_ge(multiplied, (D8 + n) * 8 + 4 * (side + 1))
                dve.wait_ge(sig_ready, 4 * n + 4)
                for m in range(MT):
                    g = gates[:, m, bass.ds(side * D_MODEL + n * CW, CW)]
                    nc.vector.tensor_tensor(g, g, acc[:, side, m, :], ALU.mult).then_inc(acc_free[side], 1)

            def gate_sum(n):
                if not (isinstance(n, int) and n == 0):
                    dve.wait_ge(turned, PC_D + 2 * n)
                dve.wait_ge(acc_free[1], 2 * (U_D[1] + 1 + n))
                for m in range(MT):
                    nc.vector.tensor_tensor(stage[:, m, :], gates[:, m, bass.ds(n * CW, CW)],
                                            gates[:, m, bass.ds(D_MODEL + n * CW, CW)],
                                            ALU.add).then_inc(z_ready, 1)

            def z_piece_lo(n):
                plain_lo(PC_D + 2 * (n - 1), NO_SPLIT,
                         lambda m: z_hi[:, bass.ds(4 * (n - 1), 4), m * P:(m + 1) * P],
                         lambda m: z_lo[:, bass.ds(4 * (n - 1), 4), m * P:(m + 1) * P])
            steps(D8, 8, {1: lambda: o_quarters(2), 3: lambda: o_quarters(3),
                          6: lambda: gate_side(0, 0)})
            gate_side(1, 0)
            gate_sum(0)
            with dve.Fori(1, NG) as n:
                steps(D8 + n, 8, {6: lambda: z_piece_lo(n), 7: lambda: gate_side(0, n)})
                gate_side(1, n)
                gate_sum(n)

            down(E8, 1, 1, 1.0, {5: lambda: z_piece_lo(NG)})
            gate_up(F8, PC_F, NO_SPLIT, U_F, 2, boundary(2))
            down(H8, 3, 2, 0.5, tail_lo(PC_F, NO_SPLIT))


_INS = ["x", "ffn1_norm_pre", "ffn1_w_in", "ffn1_w_out", "ffn1_norm_post", "mix_norm_pre", "w_in",
        "diff_lambda", "diff_subln", "swa_sinks", "w_branch_diff", "w_branch_swa", "w_out",
        "mix_norm_post", "ffn2_norm_pre", "ffn2_w_in", "ffn2_w_out", "ffn2_norm_post"]


def kernel(**inputs):
    import concourse.bacc as bacc
    from concourse.bass_utils import run_bass_kernel_spmd

    nc = bacc.Bacc("TRN2", target_bir_lowering=False, num_devices=1)
    arrays, args = {}, []
    for name in _INS:
        a = np.ascontiguousarray(inputs[name])
        arrays[f"in_{name}"] = a
        args.append(nc.dram_tensor(f"in_{name}", a.shape, mybir.dt.from_np(a.dtype), kind="ExternalInput").ap())
    out = nc.dram_tensor("out_0", (1, SEQ, D_MODEL), F32, kind="ExternalOutput").ap()
    layer_kernel(nc, *args, out)
    r = run_bass_kernel_spmd(nc, [arrays], core_ids=[0])
    return r.results[0]["out_0"]
```
